# Optimizing a Trainium2 kernel written in Bass

```python
import math
import jax, jax.numpy as jnp
from jax import lax
import numpy as np

D_MODEL = 2048
BATCH = 1
SEQ = 256
DEPTH = 2

HEAD_DIM = 128
ATTN_HEADS = 12
ATTN_WIDTH = ATTN_HEADS * HEAD_DIM
DILATION_PATTERNS = ((128, 1), (512, 4), (2048, 16))
ATTN_BLOCK = 128
CONV_WIDTH = 1536
CONV_KERNEL = 3
RET_HEADS = 12
RET_HEAD_DIM = 128
RET_WIDTH = RET_HEADS * RET_HEAD_DIM
RET_CHUNK = 128
ROPE_BASE = 10000.0
NORM_EPS = 1e-6
IN_WIDTHS = (ATTN_WIDTH, ATTN_WIDTH, ATTN_WIDTH, ATTN_WIDTH,
             CONV_WIDTH, CONV_WIDTH, CONV_WIDTH, CONV_WIDTH,
             RET_WIDTH, RET_WIDTH, RET_WIDTH, RET_WIDTH,
             D_MODEL, D_MODEL, D_MODEL)
N_IN = sum(IN_WIDTHS)

kernel_name = "hybrid_dilated_conv_retention_gated_merge"

def rms_norm(x, g):
    xf = x.astype(jnp.float32)
    y = xf * lax.rsqrt(jnp.mean(xf * xf, axis=-1, keepdims=True) + NORM_EPS)
    return (y * g.astype(jnp.float32)).astype(x.dtype)

def dilated_pattern_attn(q, k, v, window, dil):
    B, S, H, E = q.shape
    n = S // dil
    w = window // dil
    blk = math.gcd(n, ATTN_BLOCK)
    nblk = n // blk
    qs = q.reshape(B, nblk, blk, dil, H, E)
    pad = ((0, 0), (w, 0), (0, 0), (0, 0), (0, 0))
    kp = jnp.pad(k.reshape(B, n, dil, H, E), pad)
    vp = jnp.pad(v.reshape(B, n, dil, H, E), pad)
    kidx = (jnp.arange(nblk) * blk)[:, None] + jnp.arange(blk + w)[None, :]
    kb = kp[:, kidx]
    vb = vp[:, kidx]
    qpos = (jnp.arange(nblk) * blk)[:, None] + jnp.arange(blk)[None, :]
    kpos = kidx - w
    dist = qpos[:, :, None] - kpos[:, None, :]
    mask = (kpos[:, None, :] >= 0) & (dist >= 0) & (dist <= w)
    s = jnp.einsum('bnqrhe,bnkrhe->bnrhqk', qs, kb) * (E ** -0.5)
    s = jnp.where(mask[None, :, None, None], s, -jnp.inf)
    m = jnp.max(s, axis=-1)
    p = jnp.exp(s - m[..., None])
    l = jnp.sum(p, axis=-1)
    o = jnp.einsum('bnrhqk,bnkrhe->bnqrhe', p, vb)
    m_t = m.transpose(0, 1, 4, 2, 3)
    l_t = l.transpose(0, 1, 4, 2, 3)
    o = (o / l_t[..., None]).reshape(B, S, H, E)
    lse = (m_t + jnp.log(l_t)).reshape(B, S, H)
    return o, lse

def dilated_mixture_attn(q, k, v):
    q = q.astype(jnp.float32); k = k.astype(jnp.float32); v = v.astype(jnp.float32)
    outs, lses = [], []
    for window, dil in DILATION_PATTERNS:
        o, lse = dilated_pattern_attn(q, k, v, window, dil)
        outs.append(o); lses.append(lse)
    alpha = jax.nn.softmax(jnp.stack(lses, 0), axis=0)
    return jnp.einsum('gbsh,gbshe->bshe', alpha, jnp.stack(outs, 0))

def causal_short_conv(u, w, b):
    K = w.shape[0]
    S = u.shape[1]
    up = jnp.pad(u, ((0, 0), (K - 1, 0), (0, 0)))
    y = b + w[K - 1] * u
    for j in range(K - 1):
        y = y + w[j] * up[:, j:j + S]
    return y

def rotary(x, pos):
    half = x.shape[-1] // 2
    inv_freq = ROPE_BASE ** (-jnp.arange(half, dtype=jnp.float32) / half)
    ang = pos[:, None] * inv_freq[None, :]
    cos = jnp.cos(ang)[None, :, None, :]
    sin = jnp.sin(ang)[None, :, None, :]
    x1, x2 = x[..., :half], x[..., half:]
    return jnp.concatenate([x1 * cos - x2 * sin, x1 * sin + x2 * cos], axis=-1)

def retention(q, k, v):
    B, S, H, E = q.shape
    C = RET_CHUNK
    nc = S // C
    pos = jnp.arange(S, dtype=jnp.float32)
    q = rotary(q.astype(jnp.float32), pos)
    k = rotary(k.astype(jnp.float32), pos) * (E ** -0.5)
    v = v.astype(jnp.float32)
    log_gamma = jnp.log1p(-jnp.exp2(-5.0 - jnp.arange(H, dtype=jnp.float32)))
    idx = jnp.arange(C, dtype=jnp.float32)
    rel = idx[:, None] - idx[None, :]
    decay_mask = jnp.where(rel[None] >= 0,
                           jnp.exp(jnp.maximum(rel, 0.0)[None] * log_gamma[:, None, None]), 0.0)
    q_decay = jnp.exp((idx + 1.0)[None, :] * log_gamma[:, None])[None, :, :, None]
    k_decay = jnp.exp((C - 1.0 - idx)[None, :] * log_gamma[:, None])[None, :, :, None]
    chunk_decay = jnp.exp(C * log_gamma)[None, :, None, None]

    def chunks(t):
        return t.reshape(B, nc, C, H, E).transpose(1, 0, 3, 2, 4)

    def step(state, inp):
        qi, ki, vi = inp
        inner = jnp.einsum('bhqe,bhke->bhqk', qi, ki) * decay_mask[None]
        o = jnp.einsum('bhqk,bhke->bhqe', inner, vi) \
            + jnp.einsum('bhqe,bhef->bhqf', qi, state) * q_decay
        state = state * chunk_decay + jnp.einsum('bhke,bhkf->bhef', ki * k_decay, vi)
        return state, o

    state0 = jnp.zeros((B, H, E, E), jnp.float32)
    _, o = lax.scan(step, state0, (chunks(q), chunks(k), chunks(v)))
    o = o.transpose(1, 0, 3, 2, 4).reshape(B, S, H, E)
    return o * lax.rsqrt(jnp.mean(o * o, axis=-1, keepdims=True) + NORM_EPS)

def hybrid_layer(x, pre_g, post_g, w_in, conv_w, conv_b, w_branch_a, w_branch_c, w_branch_r, w_out):
    B, S, _ = x.shape
    h = rms_norm(x, pre_g)
    proj = h @ w_in
    cuts, acc = [], 0
    for wdt in IN_WIDTHS[:-1]:
        acc += wdt
        cuts.append(acc)
    (q_a, k_a, v_a, z_a, u_c, b_c, c_c, z_c,
     q_r, k_r, v_r, z_r, g_a, g_c, g_r) = jnp.split(proj, cuts, axis=-1)

    ah = lambda t: t.reshape(B, S, ATTN_HEADS, HEAD_DIM)
    o_a = dilated_mixture_attn(ah(q_a), ah(k_a), ah(v_a)).reshape(B, S, ATTN_WIDTH).astype(x.dtype)
    o_a = o_a * jax.nn.silu(z_a)
    o_c = b_c * causal_short_conv(c_c * u_c, conv_w, conv_b) * jax.nn.silu(z_c)
    rh = lambda t: t.reshape(B, S, RET_HEADS, RET_HEAD_DIM)
    o_r = retention(rh(q_r), rh(k_r), rh(v_r)).reshape(B, S, RET_WIDTH).astype(x.dtype)
    o_r = o_r * jax.nn.silu(z_r)

    merged = (jax.nn.sigmoid(g_a) * (o_a @ w_branch_a)
              + jax.nn.sigmoid(g_c) * (o_c @ w_branch_c)
              + jax.nn.sigmoid(g_r) * (o_r @ w_branch_r))
    y = merged @ w_out
    return x + rms_norm(y, post_g)

def setup_inputs(seed: int = 0) -> dict:
    key = jax.random.key(seed)
    ks = jax.random.split(key, 11)
    f32 = jnp.float32
    x = jax.random.normal(ks[0], (BATCH, SEQ, D_MODEL), f32)
    pre_norm_g = 1.0 + 0.1 * jax.random.normal(ks[1], (DEPTH, D_MODEL), f32)
    post_norm_g = 1.0 + 0.1 * jax.random.normal(ks[2], (DEPTH, D_MODEL), f32)
    w_in = jax.random.normal(ks[3], (DEPTH, D_MODEL, N_IN), f32) * (D_MODEL ** -0.5)
    conv_w = jax.random.normal(ks[4], (DEPTH, CONV_KERNEL, CONV_WIDTH), f32) * (CONV_KERNEL ** -0.5)
    conv_b = 0.02 * jax.random.normal(ks[5], (DEPTH, CONV_WIDTH), f32)
    w_branch_a = jax.random.normal(ks[6], (DEPTH, ATTN_WIDTH, D_MODEL), f32) * (ATTN_WIDTH ** -0.5)
    w_branch_c = jax.random.normal(ks[7], (DEPTH, CONV_WIDTH, D_MODEL), f32) * (CONV_WIDTH ** -0.5)
    w_branch_r = jax.random.normal(ks[8], (DEPTH, RET_WIDTH, D_MODEL), f32) * (RET_WIDTH ** -0.5)
    w_out = jax.random.normal(ks[9], (DEPTH, D_MODEL, D_MODEL), f32) * (D_MODEL ** -0.5)
    return {"x": x, "pre_norm_g": pre_norm_g, "post_norm_g": post_norm_g, "w_in": w_in,
            "conv_w": conv_w, "conv_b": conv_b, "w_branch_a": w_branch_a,
            "w_branch_c": w_branch_c, "w_branch_r": w_branch_r, "w_out": w_out}

def reference(x, pre_norm_g, post_norm_g, w_in, conv_w, conv_b, w_branch_a, w_branch_c, w_branch_r, w_out):
    for layer in range(DEPTH):
        x = hybrid_layer(x, pre_norm_g[layer], post_norm_g[layer], w_in[layer],
                         conv_w[layer], conv_b[layer], w_branch_a[layer],
                         w_branch_c[layer], w_branch_r[layer], w_out[layer])
    return x


_drawn_inputs = setup_inputs


def setup_inputs(seed=0):
    import zlib

    import numpy as np

    out = dict(_drawn_inputs(seed))
    spreads = {}
    factors = {'conv_b': 3.398}
    for name, (base, spread) in spreads.items():
        noise = np.random.default_rng([zlib.crc32(name.encode()), seed]).standard_normal(out[name].shape)
        drawn = base * np.exp(spread * noise) if base else spread * noise
        out[name] = __import__('jax').numpy.asarray(drawn.astype(out[name].dtype))
    for name, factor in factors.items():
        out[name] = (out[name] * factor).astype(out[name].dtype)
    return out
```

```python
import math
from contextlib import ExitStack

import numpy as np

import concourse.bass as bass
from concourse import mybir

F32 = mybir.dt.float32
F32R = mybir.dt.float32r
ALU = mybir.AluOpType
ACT = mybir.ActivationFunctionType
AX_X = mybir.AxisListType.X

P = 128
DEPTH = 2
D_MODEL = 2048
SEQ = 256
TILES = SEQ // P
WIDTH = 1536
HEADS = WIDTH // P
DILATIONS = ((128, 1), (512, 4), (2048, 16))
ROPE_BASE = 10000.0
EPS = 1e-6

COLS = 512
HPB = COLS // P
GROUPS = WIDTH // COLS
OUT_BLOCKS = D_MODEL // COLS
KT = D_MODEL // P
KT_MIX = WIDTH // P
CHUNK = 4
HALF = 2
RAW_SLOTS = 4
SPLIT_SLOTS = 4
SIDE_BANKS = 4
MIXERS = ("attention", "conv", "retention")

SECTION = {"attention": {"q": 0, "k": 1, "v": 2, "z": 3},
           "conv": {"u": 4, "b": 5, "c": 6, "z": 7},
           "retention": {"q": 8, "k": 9, "v": 10, "z": 11}}
ROLES = {"attention": "vqkz", "conv": "ucbz", "retention": "vqkz"}
GATES_AT = 12 * GROUPS

STEPS = {"attention": TILES + TILES + HPB + HPB + HPB // 2 + TILES,
         "conv": TILES + TILES,
         "retention": TILES + TILES + HPB + HPB // 2 + TILES}
X_STEPS = TILES * KT // HPB
MERGE_STEPS = TILES * OUT_BLOCKS

CONST_PARTS = (("ident", P), ("log_count", 3 * P), ("causal", 3 * P), ("cos", TILES * 64),
               ("sin", TILES * 64), ("neg_sin", TILES * 64), ("gamma_q", TILES * HEADS),
               ("gamma_v", TILES * HEADS))
CONST_AT, CONST_COLS = {}, 0
for _name, _n in CONST_PARTS:
    CONST_AT[_name] = (CONST_COLS, CONST_COLS + _n)
    CONST_COLS += _n
PARAM_COLS = KT + 4 * KT_MIX


def layer_blocks():
    blocks = []
    for b, mixer in enumerate(MIXERS):
        for g in range(GROUPS):
            for role in ROLES[mixer]:
                blocks.append(("w_in", COLS * (GROUPS * SECTION[mixer][role] + g), KT,
                               ("mix", mixer, role, g)))
        for j in range(OUT_BLOCKS):
            blocks.append(("w_in", COLS * (GATES_AT + OUT_BLOCKS * b + j), KT, ("gate", mixer, "", j)))
        for j in range(OUT_BLOCKS):
            blocks.append((mixer, COLS * j, KT_MIX, ("branch", mixer, "", j)))
    for j in range(OUT_BLOCKS):
        blocks.append(("w_out", COLS * j, KT, ("out", "", "", j)))
    return blocks


BLOCKS = layer_blocks()
NBLOCKS = len(BLOCKS)
FIRST_HALF = [0]
for _b in BLOCKS:
    FIRST_HALF.append(FIRST_HALF[-1] + _b[2] // HALF)
HALVES = FIRST_HALF[-1]
CHUNKS = HALVES * HALF // CHUNK
BLOCK_OF = [n for n, _b in enumerate(BLOCKS) for _ in range(_b[2] // HALF)]
PER_BLOCK_GROUP = len(ROLES["attention"])
MIXER_BLOCKS = PER_BLOCK_GROUP * GROUPS + 2 * OUT_BLOCKS

AHEAD = SPLIT_SLOTS


def first_block(mixer, g):
    return MIXER_BLOCKS * MIXERS.index(mixer) + PER_BLOCK_GROUP * g


def step0(mixer, g):
    before = X_STEPS
    for m in MIXERS[:MIXERS.index(mixer)]:
        before += GROUPS * STEPS[m]
    return before + g * STEPS[mixer]


MERGE_STEP0 = step0("retention", GROUPS)
SIDE_STEPS = MERGE_STEP0 + MERGE_STEPS
assert NBLOCKS % 2 == 0 and SIDE_STEPS % SIDE_BANKS == 0
assert HALVES % SPLIT_SLOTS == 0 and CHUNKS % RAW_SLOTS == 0

B = KT // HALF


def due(table, offset=0):
    out = {}
    for mixer, whats in table.items():
        for g in range(GROUPS):
            for what, at in whats:
                out.setdefault(FIRST_HALF[first_block(mixer, g)] + at + offset, []).append((what, mixer, g))
    return out


PE_DUE = due({
    "attention": [("q", 2 * B + 3), ("k", 3 * B + 2), ("scores", 3 * B + 4), ("probs", 4 * B + 2),
                  ("values", 4 * B + 4), ("out", 4 * B + 6)],
    "conv": [("prod", 2 * B + 2), ("out", 4 * B + 2)],
    "retention": [("q", 2 * B + 3), ("k", 3 * B + 3), ("scores", 3 * B + 5), ("values", 4 * B + 1),
                  ("out", 4 * B + 6)]})
ACT_DUE = due({
    "attention": [("q", 2 * B + 3), ("k", 3 * B + 2), ("exp", 3 * B + 5), ("probs", 4 * B + 2),
                  ("out", 4 * B + 6)],
    "conv": [("prod", 2 * B + 2), ("out", 4 * B + 2)],
    "retention": [("q", 2 * B + 3), ("k", 3 * B + 3), ("square", 4 * B + 1), ("out", 4 * B + 6)]}, AHEAD)
DVE_DUE = due({
    "attention": [("scores", 3 * B + 4), ("sums", 4 * B + 1), ("values", 4 * B + 4), ("out", 4 * B + 6)],
    "conv": [("conv0", 2 * B + 3), ("conv1", 2 * B + 4), ("conv2", 2 * B + 5), ("gate", 4 * B),
             ("out", 4 * B + 2)],
    "retention": [("scores", 3 * B + 5), ("values", 4 * B + 1), ("norm", 4 * B + 2),
                  ("gate", 4 * B + 3), ("out", 4 * B + 6)]}, AHEAD)
EVICT_DUE = {FIRST_HALF[n + 1] - 1 + AHEAD: n for n in range(NBLOCKS)}
MERGE_BLOCK0 = first_block("retention", GROUPS) + OUT_BLOCKS
MERGE_DUE = {FIRST_HALF[MERGE_BLOCK0 + j + 1] + 2: j for j in range(OUT_BLOCKS)}
MERGE_DRAIN_DUE = {h + AHEAD: j for h, j in MERGE_DUE.items()}


def build(nc, x, w_in, w_attention, w_conv, w_retention, w_out, post_g, params, consts, out):
    weights = {
        "w_in": w_in.rearrange("l (k p) n -> p (l k) n", p=P),
        "attention": w_attention.rearrange("l (k p) n -> p (l k) n", p=P),
        "conv": w_conv.rearrange("l (k p) n -> p (l k) n", p=P),
        "retention": w_retention.rearrange("l (k p) n -> p (l k) n", p=P),
        "w_out": w_out.rearrange("l (k p) n -> p (l k) n", p=P),
    }
    x_rows = x.rearrange("(t p) d -> p t d", p=P)
    out_rows = out.rearrange("(t p) d -> p t d", p=P)

    with ExitStack() as ctx:
        def sb(name, shape, dt=F32):
            return ctx.enter_context(nc.sbuf_tensor(name, shape, dt))

        def sem(name):
            return ctx.enter_context(nc.semaphore(name))

        raw = sb("raw", [P, RAW_SLOTS, CHUNK * COLS])
        w_lead = sb("w_lead", [P, SPLIT_SLOTS, HALF * COLS], F32R)
        w_trail = sb("w_trail", [P, SPLIT_SLOTS, HALF * COLS], F32R)
        hT_lead = sb("hT_lead", [P, KT, SEQ], F32R)
        hT_trail = sb("hT_trail", [P, KT, SEQ], F32R)
        oT_lead = sb("oT_lead", [P, KT_MIX, SEQ], F32R)
        oT_trail = sb("oT_trail", [P, KT_MIX, SEQ], F32R)
        merged = sb("merged", [P, TILES, D_MODEL])
        gates = sb("gates", [P, TILES, D_MODEL])
        post_gain = sb("post_gain", [P, D_MODEL])
        v_sb = sb("v_sb", [P, TILES, COLS])
        q_sb = sb("q_sb", [P, TILES, COLS])
        k_sb = sb("k_sb", [P, TILES, COLS])
        z_sb = sb("z_sb", [P, TILES, COLS])
        qT = sb("qT", [P, HPB, SEQ])
        kT = sb("kT", [P, HPB, SEQ])
        prodT = sb("prodT", [P, HPB, 2 + SEQ])
        probs = sb("probs", [P, HPB, 3 * P])
        probsT = sb("probsT", [P, HPB, 3 * P])
        par = sb("par", [P, PARAM_COLS])
        cst = sb("cst", [P, CONST_COLS])
        stat = sb("stat", [P, 64])
        exponent = sb("exponent", [P, 8])

        ps = [ctx.enter_context(nc.psum_tensor(f"ps{i}", [P, COLS], F32)) for i in range(8)]

        def const(name):
            a, b = CONST_AT[name]
            return cst[:, a:b]

        ident = const("ident")
        gamma_q = const("gamma_q").rearrange("p (h t) -> p h t", t=TILES)
        gamma_v = const("gamma_v").rearrange("p (h t) -> p h t", t=TILES)
        rope = {n: const(n).rearrange("p (t f) -> p t f", t=TILES) for n in ("cos", "sin", "neg_sin")}
        pre_gain = par[:, 0:KT]
        tap = [par[:, KT + i * KT_MIX:KT + (i + 1) * KT_MIX] for i in range(3)]
        conv_bias = par[:, KT + 3 * KT_MIX:KT + 4 * KT_MIX]

        x_ssq, x_rstd = stat[:, 0:2], stat[:, 2:4]
        y_ssq, y_sum, y_rstd = stat[:, 4:12], stat[:, 12:14], stat[:, 14:16]
        neg_max, row_sum, row_inv = stat[:, 16:24], stat[:, 24:32], stat[:, 32:40]
        o_ssq, o_rstd = stat[:, 40:48], stat[:, 48:56]

        work = probs[:, :, :].rearrange("p h c -> p (h c)")
        work2 = work[:, 0:2 * COLS].rearrange("p (s c) -> p s c", s=2)
        ret_o = work[:, 0:HPB * TILES * P].rearrange("p (h t e) -> p h t e", h=HPB, t=TILES)

        raw_in = [sem(f"raw_in{i}") for i in range(RAW_SLOTS)]
        lead_ready = sem("lead_ready")
        trail_ready = sem("trail_ready")
        half_done = sem("half_done")
        evicted = [sem(f"evicted{i}") for i in range(2)]
        side_ready = sem("side_ready")
        drained = [sem(f"drained{i}") for i in range(SIDE_BANKS)]
        loads_in = sem("loads_in")
        zeroed = sem("zeroed")
        params_in = sem("params_in")
        x_new = sem("x_new")
        x_squared = sem("x_squared")
        x_mean = sem("x_mean")
        x_rstd_ready = sem("x_rstd_ready")
        xn_ready = sem("xn_ready")
        x_lead = sem("x_lead")
        x_trail = sem("x_trail")
        sig_ready = sem("sig_ready")
        rotated = sem("rotated")
        maxes = sem("maxes")
        neg_max_ready = sem("neg_max_ready")
        exp_ready = sem("exp_ready")
        inv_ready = sem("inv_ready")
        conv_steps = sem("conv_steps")
        conv_gated = sem("conv_gated")
        conv_trail = sem("conv_trail")
        o_squared = sem("o_squared")
        o_ssq_ready = sem("o_ssq_ready")
        o_mean = sem("o_mean")
        o_rstd_ready = sem("o_rstd_ready")
        ret_gated = sem("ret_gated")
        out_lead = sem("out_lead")
        merged_ready = sem("merged_ready")
        y_squared = sem("y_squared")
        y_sum_ready = sem("y_sum_ready")
        y_mean = sem("y_mean")
        y_rstd_ready = sem("y_rstd_ready")
        residual_in = sem("residual_in")
        residual_out = sem("residual_out")
        sp_passed = sem("sp_passed")
        pool_passed = sem("pool_passed")

        def chunk_landed(l, i):
            return raw_in[i % RAW_SLOTS], l * (16 * CHUNKS // RAW_SLOTS) + 16 * (i // RAW_SLOTS + 1)

        def done_half(l, h):
            return half_done, l * HALVES + (SPLIT_SLOTS + h + 1)

        def done_block(l, n):
            return done_half(l, FIRST_HALF[n + 1] - 1)

        def moved_out(l, n):
            return evicted[n % 2], l * (TILES * NBLOCKS // 2) + TILES * (n // 2 + 2)

        def bank_free(l, n):
            return evicted[n % 2], l * (TILES * NBLOCKS // 2) + TILES * (n // 2 + 1)

        def step_ready(l, m):
            return side_ready, l * SIDE_STEPS + (m + 1)

        def step_drained(l, m):
            return drained[m % SIDE_BANKS], l * (SIDE_STEPS // SIDE_BANKS) + (m // SIDE_BANKS + 2)

        def side_bank_free(l, m):
            return drained[m % SIDE_BANKS], l * (SIDE_STEPS // SIDE_BANKS) + (m // SIDE_BANKS + 1)

        def count(semaphore, per_layer):
            return lambda l, n: (semaphore, l * per_layer + n)

        group_no = {(m, g): GROUPS * i + g for i, m in enumerate(MIXERS) for g in range(GROUPS)}
        sig_tiles = count(sig_ready, TILES * 3 * GROUPS)
        rotated_tiles = count(rotated, 2 * TILES * GROUPS)
        lead_steps = count(out_lead, TILES * 3 * GROUPS + MERGE_STEPS)
        merged_tiles = count(merged_ready, 2 * TILES * OUT_BLOCKS)

        def lead_no(mixer, g, t):
            return TILES * group_no[mixer, g] + t + 1

        def merge_lead_no(j, t):
            return TILES * 3 * GROUPS + TILES * j + t + 1

        def bank(n, t):
            return ps[2 * (n % 2) + t]

        def side(m):
            return ps[4 + m % SIDE_BANKS]

        def tok(t):
            return slice(t * P, (t + 1) * P)

        def head(h):
            return slice(h * P, (h + 1) * P)

        def heads4(ap):
            return ap.rearrange("p (h c) -> p h c", h=HPB)

        block = ctx.enter_context(nc.Block())

        @block.sync
        def _(sp):
            sp.dma_start(gates[:, :, :], x_rows).then_inc(loads_in, 16)
            sp.dma_start(cst[:, :], consts).then_inc(loads_in, 16)
            with sp.Fori(0, DEPTH) as l:
                for n, (name, col, tiles, _what) in enumerate(BLOCKS):
                    for c in range(tiles // CHUNK):
                        i = FIRST_HALF[n] * HALF // CHUNK + c
                        sp.wait_ge(trail_ready, l * HALVES + (2 * i + 2))
                        sp.sem_inc(sp_passed, 1)
                        sp.dma_start(
                            raw[:, i % RAW_SLOTS, :].rearrange("p (k n) -> p k n", k=CHUNK),
                            weights[name][:, bass.ds(l * tiles + c * CHUNK, CHUNK), col:col + COLS],
                        ).then_inc(raw_in[i % RAW_SLOTS], 16)

        @block.gpsimd
        def _(pool):
            def wait(semaphore, value):
                pool.wait_ge(semaphore, value)
                pool.sem_inc(pool_passed, 1)

            def rstd(src, mean_sem, mean_value, dst, width, n):
                pool.tensor_scalar(dst, src, 1.0 / width, EPS, ALU.mult, ALU.add).then_inc(mean_sem, 1)
                pool.wait_ge(mean_sem, mean_value)
                return pool.tensor_tensor(dst, dst, exponent[:, 0:n], ALU.pow)

            pool.memset(exponent[:, :], -0.5).then_inc(zeroed, 1)
            pool.memset(prodT[:, :, 0:2], 0.0).then_inc(zeroed, 1)
            pool.wait_ge(zeroed, 2)
            pool.dma_start(out, x).then_inc(residual_out, 16)
            with pool.Fori(0, DEPTH) as l:
                wait(x_new, l * TILES + TILES)
                pool.dma_start(par[:, :], params[:, bass.ds(l * PARAM_COLS, PARAM_COLS)]).then_inc(params_in, 16)
                pool.dma_start(post_gain[:, :], post_g[bass.ds(l, 1), :].to_broadcast((P, D_MODEL))).then_inc(params_in, 16)
                wait(x_squared, l * TILES + TILES)
                rstd(x_ssq, x_mean, l + 1, x_rstd, D_MODEL, 2).then_inc(x_rstd_ready, 1)
                for g in range(GROUPS):
                    wait(o_ssq_ready, l * GROUPS + (g + 1))
                    rstd(o_ssq, o_mean, l * GROUPS + (g + 1), o_rstd, P, 8).then_inc(o_rstd_ready, 1)
                wait(*merged_tiles(l, 2 * TILES * OUT_BLOCKS))
                wait(residual_out, l * 16 + 16)
                pool.dma_start(gates[:, :, :], out_rows).then_inc(residual_in, 16)
                wait(y_sum_ready, l + 1)
                rstd(y_sum, y_mean, l + 1, y_rstd, D_MODEL, 2).then_inc(y_rstd_ready, 1)
                wait(x_new, l * TILES + 2 * TILES)
                pool.dma_start(out_rows, gates[:, :, :]).then_inc(residual_out, 16)
            pool.wait_ge(residual_out, 16 * (DEPTH + 1))

        @block.tensor
        def _(pe):
            def transposes(l, m, sources):
                pe.wait_ge(*side_bank_free(l, m))
                for i, s in enumerate(sources):
                    last = pe.transpose(side(m)[:, head(i)], s, ident)
                last.then_inc(side_ready, 1)

            def side_steps(l, what, mixer, g):
                m = step0(mixer, g)
                n0 = first_block(mixer, g)
                if what in ("q", "k"):
                    i = "qk".index(what)
                    if mixer == "attention":
                        pe.wait_ge(*moved_out(l, n0 + 1 + i))
                    else:
                        pe.wait_ge(*rotated_tiles(l, TILES * (2 * g + i + 1)))
                    src = (q_sb, k_sb)[i]
                    for t in range(TILES):
                        transposes(l, m + TILES * i + t, [src[:, t, head(h)] for h in range(HPB)])
                elif what == "prod":
                    pe.wait_ge(*moved_out(l, n0 + 1))
                    for t in range(TILES):
                        transposes(l, m + t, [q_sb[:, t, head(h)] for h in range(HPB)])
                elif what == "scores":
                    for i in range(2 * TILES):
                        pe.wait_ge(*step_drained(l, m + i))
                    for h in range(HPB):
                        s = m + 2 * TILES + h
                        pe.wait_ge(*side_bank_free(l, s))
                        if mixer == "attention":
                            pe.matmul(side(s)[:, 0:P], qT[:, h, 0:P], kT[:, h, 0:P], start=True, stop=True)
                            pe.matmul(side(s)[:, P:3 * P], qT[:, h, P:SEQ], kT[:, h, :],
                                      start=True, stop=True).then_inc(side_ready, 1)
                        else:
                            pe.matmul(side(s)[:, 0:SEQ], kT[:, h, 0:P], qT[:, h, :], start=True, stop=True)
                            pe.matmul(side(s)[:, SEQ:3 * P], kT[:, h, P:SEQ], qT[:, h, P:SEQ],
                                      start=True, stop=True).then_inc(side_ready, 1)
                elif what == "probs":
                    for h in range(HPB):
                        s = m + 2 * TILES + HPB + h
                        pe.wait_ge(exp_ready, l * (HPB * GROUPS) + (HPB * g + h + 1))
                        pe.wait_ge(*side_bank_free(l, s))
                        for i in range(3):
                            last = pe.transpose(side(s)[:, head(i)], probs[:, h, head(i)], ident)
                        last.then_inc(side_ready, 1)
                elif what == "values":
                    pe.wait_ge(*moved_out(l, n0))
                    s0 = m + STEPS[mixer] - TILES - HPB // 2
                    for i in range(HPB):
                        pe.wait_ge(*step_drained(l, s0 - HPB + i))
                    for i in range(HPB // 2):
                        pe.wait_ge(*side_bank_free(l, s0 + i))
                        for hh in range(2):
                            h = 2 * i + hh
                            o = side(s0 + i)[:, 2 * hh * P:(2 * hh + 2) * P]
                            pe.matmul(o[:, 0:P], probsT[:, h, 0:P], v_sb[:, 0, head(h)], start=True, stop=True)
                            pe.matmul(o[:, P:2 * P], probsT[:, h, P:2 * P], v_sb[:, 0, head(h)],
                                      start=True, stop=False)
                            last = pe.matmul(o[:, P:2 * P], probsT[:, h, 2 * P:3 * P], v_sb[:, 1, head(h)],
                                             start=False, stop=True)
                        last.then_inc(side_ready, 1)
                elif what == "out":
                    s0 = m + STEPS[mixer] - TILES
                    if mixer == "attention":
                        for i in range(HPB // 2):
                            pe.wait_ge(*step_drained(l, s0 - HPB // 2 + i))
                    elif mixer == "conv":
                        pe.wait_ge(conv_gated, l * (TILES * GROUPS) + TILES * (g + 1))
                    else:
                        pe.wait_ge(ret_gated, l * GROUPS + (g + 1))
                    for t in range(TILES):
                        transposes(l, s0 + t, [z_sb[:, t, head(h)] for h in range(HPB)])

            def wait_stationary(l, n, k):
                kind, mixer, _role, j = BLOCKS[n][3]
                if n == 0 and k == 0:
                    pe.wait_ge(x_trail, l * X_STEPS + X_STEPS)
                elif kind == "branch" and j == 0 and k == 0:
                    if mixer == "conv":
                        pe.wait_ge(conv_trail, l * (TILES * GROUPS) + TILES * GROUPS)
                    else:
                        s = step0(mixer, GROUPS - 1) + STEPS[mixer] - TILES
                        for t in range(TILES):
                            pe.wait_ge(*step_drained(l, s + t))
                elif kind == "out" and j == 0 and k % HPB == 0:
                    for t in range(TILES):
                        pe.wait_ge(*step_drained(l, MERGE_STEP0 + TILES * (k // HPB) + t))

            def multiply(l, h):
                n = BLOCK_OF[h]
                kind = BLOCKS[n][3][0]
                lead, trail = (oT_lead, oT_trail) if kind == "branch" else (hT_lead, hT_trail)
                slot = h % SPLIT_SLOTS
                k0 = HALF * (h - FIRST_HALF[n])
                wait_stationary(l, n, k0)
                if k0 == 0:
                    pe.wait_ge(*bank_free(l, n))
                pe.wait_ge(trail_ready, l * HALVES + (2 * RAW_SLOTS + h + 1))
                for i in range(HALF):
                    k = k0 + i
                    wl = w_lead[:, slot, i * COLS:(i + 1) * COLS]
                    wt = w_trail[:, slot, i * COLS:(i + 1) * COLS]
                    for t in range(TILES):
                        acc = bank(n, t)[:, :]
                        pe.matmul(acc, lead[:, k, tok(t)], wl, start=(k == 0), stop=False)
                        pe.matmul(acc, lead[:, k, tok(t)], wt, start=False, stop=False)
                        last = pe.matmul(acc, trail[:, k, tok(t)], wl, start=False,
                                         stop=(k == BLOCKS[n][2] - 1))
                last.then_inc(half_done, 1)

            pe.wait_ge(loads_in, 32)
            with pe.Fori(0, DEPTH) as l:
                for m in range(X_STEPS):
                    t, c = divmod(m, KT // HPB)
                    pe.wait_ge(xn_ready, l * TILES + (t + 1))
                    transposes(l, m, [merged[:, t, head(HPB * c + i)] for i in range(HPB)])
                for h in range(HALVES):
                    multiply(l, h)
                    for what, mixer, g in PE_DUE.get(h, []):
                        side_steps(l, what, mixer, g)
                    if h in MERGE_DUE:
                        j = MERGE_DUE[h]
                        pe.wait_ge(*merged_tiles(l, TILES * (OUT_BLOCKS + j + 1)))
                        for t in range(TILES):
                            transposes(l, MERGE_STEP0 + TILES * j + t,
                                       [merged[:, t, head(HPB * j + i)] for i in range(HPB)])

        @block.scalar
        def _(act):
            def split_lead(l, h):
                i = h * HALF // CHUNK
                part = (h * HALF % CHUNK) * COLS
                if part == 0:
                    act.wait_ge(*chunk_landed(l, i))
                act.wait_ge(half_done, l * HALVES + (h + 1))
                act.activation(w_lead[:, h % SPLIT_SLOTS, :], raw[:, i % RAW_SLOTS, part:part + HALF * COLS],
                               ACT.Copy).then_inc(lead_ready, 1)

            def evict(l, n):
                kind, mixer, role, j = BLOCKS[n][3]
                if kind == "mix":
                    copy_to = {("attention", "v"): v_sb, ("attention", "q"): q_sb, ("attention", "k"): k_sb,
                               ("conv", "u"): v_sb, ("conv", "b"): k_sb}.get((mixer, role))
                    if copy_to is not None:
                        act.wait_ge(*done_block(l, n))
                        for t in range(TILES):
                            act.activation(copy_to[:, t, :], bank(n, t)[:, :], ACT.Copy).then_inc(evicted[n % 2], 1)
                    elif role == "z":
                        act.wait_ge(*done_block(l, n))
                        for t in range(TILES):
                            act.activation(z_sb[:, t, :], bank(n, t)[:, :], ACT.Sigmoid).then_inc(sig_ready, 1)
                elif kind == "gate":
                    act.wait_ge(*done_block(l, n))
                    if mixer == MIXERS[0] and j == 0:
                        act.wait_ge(residual_out, l * 16 + 16)
                    for t in range(TILES):
                        act.activation(gates[:, t, COLS * j:COLS * (j + 1)], bank(n, t)[:, :],
                                       ACT.Sigmoid).then_inc(evicted[n % 2], 1)
                elif kind == "out":
                    act.wait_ge(*done_block(l, n))
                    for t in range(TILES):
                        act.activation(z_sb[:, t, :], bank(n, t)[:, :], ACT.Square,
                                       accum_out=y_ssq[:, OUT_BLOCKS * t + j:OUT_BLOCKS * t + j + 1]).then_inc(y_squared, 1)

            def lead_of_step(l, s, dst):
                act.wait_ge(*step_ready(l, s))
                act.activation(dst, heads4(side(s)[:, :]), ACT.Copy).then_inc(out_lead, 1)

            def side_work(l, what, mixer, g):
                m = step0(mixer, g)
                if what in ("q", "k", "prod"):
                    i = 1 if what == "k" else 0
                    for t in range(TILES):
                        s = m + TILES * i + t
                        dst = prodT[:, :, 2 + t * P:2 + (t + 1) * P] if what == "prod" else (qT, kT)[i][:, :, tok(t)]
                        act.wait_ge(*step_ready(l, s))
                        act.activation(dst, heads4(side(s)[:, :]), ACT.Copy).then_inc(drained[s % SIDE_BANKS], 1)
                elif what == "exp":
                    act.wait_ge(neg_max_ready, l * GROUPS + (g + 1))
                    for h in range(HPB):
                        for t, cols in ((0, slice(0, P)), (1, slice(P, 3 * P))):
                            c = TILES * h + t
                            last = act.activation(probs[:, h, cols], probs[:, h, cols], ACT.Exp,
                                                  bias=neg_max[:, c:c + 1], accum_out=row_sum[:, c:c + 1])
                        last.then_inc(exp_ready, 1)
                elif what == "probs":
                    for h in range(HPB):
                        s = m + 2 * TILES + HPB + h
                        act.wait_ge(*step_ready(l, s))
                        act.activation(probsT[:, h, :], side(s)[:, 0:3 * P], ACT.Copy).then_inc(drained[s % SIDE_BANKS], 1)
                elif what == "square":
                    s0 = m + STEPS[mixer] - TILES - HPB // 2
                    for i in range(HPB // 2):
                        act.wait_ge(*step_drained(l, s0 + i))
                    act.activation(q_sb[:, :, :].rearrange("p a c -> p (a c)"),
                                   ret_o.rearrange("p h t e -> p (h t e)"), ACT.Square).then_inc(o_squared, 1)
                elif what == "out":
                    s0 = m + STEPS[mixer] - TILES
                    for t in range(TILES):
                        dst = oT_lead[:, HPB * g:HPB * (g + 1), tok(t)]
                        if mixer == "conv":
                            act.wait_ge(*step_drained(l, s0 + t))
                            act.activation(dst, heads4(work2[:, t, :]), ACT.Copy).then_inc(out_lead, 1)
                        else:
                            lead_of_step(l, s0 + t, dst)

            act.wait_ge(loads_in, 32)
            with act.Fori(0, DEPTH) as l:
                for t in range(TILES):
                    act.wait_ge(x_new, l * TILES + TILES)
                    act.activation(merged[:, t, :], gates[:, t, :], ACT.Square,
                                   accum_out=x_ssq[:, t:t + 1]).then_inc(x_squared, 1)
                for m in range(X_STEPS):
                    t, c = divmod(m, KT // HPB)
                    act.wait_ge(*step_drained(l, m))
                    act.activation(hT_lead[:, HPB * c:HPB * (c + 1), tok(t)], heads4(work2[:, m % 2, :]),
                                   ACT.Copy).then_inc(x_lead, 1)
                for h in range(HALVES + AHEAD):
                    if h < HALVES:
                        split_lead(l, h)
                    if h in EVICT_DUE:
                        evict(l, EVICT_DUE[h])
                    for what, mixer, g in ACT_DUE.get(h, []):
                        side_work(l, what, mixer, g)
                    if h in MERGE_DRAIN_DUE:
                        j = MERGE_DRAIN_DUE[h]
                        for t in range(TILES):
                            lead_of_step(l, MERGE_STEP0 + TILES * j + t, hT_lead[:, HPB * j:HPB * (j + 1), tok(t)])

        @block.vector
        def _(dve):
            def split_trail(l, h):
                i = h * HALF // CHUNK
                part = (h * HALF % CHUNK) * COLS
                s = h % SPLIT_SLOTS
                dve.wait_ge(lead_ready, l * HALVES + (h + 1))
                dve.tensor_tensor(w_trail[:, s, :], raw[:, i % RAW_SLOTS, part:part + HALF * COLS],
                                  w_lead[:, s, :].bitcast(F32), ALU.subtract).then_inc(trail_ready, 1)

            def rotate(l, n, g, role):
                dst = q_sb if role == "q" else k_sb
                dve.wait_ge(*done_block(l, n))
                for t in range(TILES):
                    src = bank(n, t)[:, :].rearrange("p (h s f) -> p h s f", h=HPB, s=2)
                    cos_part = work2[:, 0, :].rearrange("p (h s f) -> p h s f", h=HPB, s=2)
                    sin_part = work2[:, 1, :].rearrange("p (h s f) -> p h s f", h=HPB, s=2)
                    if t > 0:
                        dve.wait_ge(*rotated_tiles(l, TILES * (2 * g + "qk".index(role)) + t))
                    for s in range(2):
                        table = rope["neg_sin" if s == 0 else "sin"][:, t, :]
                        dve.tensor_tensor(sin_part[:, :, s, :], src[:, :, 1 - s, :],
                                          table.unsqueeze(1).to_broadcast((P, HPB, 64)), ALU.mult)
                    cos = rope["cos"][:, t, :].unsqueeze(1).unsqueeze(1).to_broadcast((P, HPB, 2, 64))
                    dve.tensor_tensor(cos_part, src, cos, ALU.mult).then_inc(evicted[n % 2], 1)
                    dve.wait_ge(evicted[n % 2], l * (TILES * NBLOCKS // 2) + (TILES * (n // 2 + 1) + t + 1))
                    dve.tensor_tensor(dst[:, t, :], work2[:, 0, :], work2[:, 1, :], ALU.add).then_inc(rotated, 1)

            def evict(l, n):
                kind, mixer, role, j = BLOCKS[n][3]
                if kind == "mix" and role == "z":
                    for t in range(TILES):
                        dve.wait_ge(*sig_tiles(l, TILES * group_no[mixer, j] + t + 1))
                        dve.tensor_tensor(z_sb[:, t, :], bank(n, t)[:, :], z_sb[:, t, :],
                                          ALU.mult).then_inc(evicted[n % 2], 1)
                elif kind == "mix" and mixer == "retention" and role in "qk":
                    rotate(l, n, j, role)
                elif kind == "mix" and mixer == "retention":
                    dve.wait_ge(*done_block(l, n))
                    for t in range(TILES):
                        gv = gamma_v[:, HPB * j:HPB * (j + 1), t].unsqueeze(2).to_broadcast((P, HPB, P))
                        dve.tensor_tensor(heads4(v_sb[:, t, :]), heads4(bank(n, t)[:, :]), gv,
                                          ALU.mult).then_inc(evicted[n % 2], 1)
                elif kind == "mix" and role == "c":
                    dve.wait_ge(*moved_out(l, n - 1))
                    dve.wait_ge(*done_block(l, n))
                    for t in range(TILES):
                        dve.tensor_tensor(q_sb[:, t, :], bank(n, t)[:, :], v_sb[:, t, :],
                                          ALU.mult).then_inc(evicted[n % 2], 1)
                elif kind == "branch":
                    b = MIXERS.index(mixer)
                    cols = slice(COLS * j, COLS * (j + 1))
                    dve.wait_ge(*moved_out(l, n - OUT_BLOCKS))
                    dve.wait_ge(*done_block(l, n))
                    for t in range(TILES):
                        dst = merged if b == 0 else gates
                        dve.tensor_tensor(dst[:, t, cols], bank(n, t)[:, :], gates[:, t, cols],
                                          ALU.mult).then_inc(evicted[n % 2], 1)
                    if b > 0:
                        dve.wait_ge(*moved_out(l, n))
                        for t in range(TILES):
                            dve.tensor_tensor(merged[:, t, cols], merged[:, t, cols], gates[:, t, cols],
                                              ALU.add).then_inc(merged_ready, 1)
                elif kind == "out":
                    if j == 0:
                        dve.wait_ge(*step_ready(l, MERGE_STEP0 + MERGE_STEPS - 1))
                        dve.wait_ge(params_in, l * 32 + 32)
                    for t in range(TILES):
                        dve.wait_ge(y_squared, l * (TILES * OUT_BLOCKS) + (TILES * j + t + 1))
                        dve.tensor_tensor(merged[:, t, COLS * j:COLS * (j + 1)], bank(n, t)[:, :],
                                          post_gain[:, COLS * j:COLS * (j + 1)], ALU.mult).then_inc(evicted[n % 2], 1)

            def trail_of_step(l, s, lead_count, lead, dst):
                dve.wait_ge(*lead_steps(l, lead_count))
                dve.tensor_tensor(dst, heads4(side(s)[:, :]), lead.bitcast(F32),
                                  ALU.subtract).then_inc(drained[s % SIDE_BANKS], 1)

            def side_work(l, what, mixer, g):
                m = step0(mixer, g)
                n0 = first_block(mixer, g)
                if what == "scores":
                    for h in range(HPB):
                        s = m + 2 * TILES + h
                        dve.wait_ge(*step_ready(l, s))
                        if mixer == "attention":
                            dve.scalar_tensor_tensor(probs[:, h, :], side(s)[:, 0:3 * P], P ** -0.5,
                                                     const("log_count"), ALU.mult, ALU.add).then_inc(drained[s % SIDE_BANKS], 1)
                        else:
                            dve.tensor_tensor(probsT[:, h, :], side(s)[:, 0:3 * P], const("causal"),
                                              ALU.mult).then_inc(drained[s % SIDE_BANKS], 1)
                    if mixer == "attention":
                        for h in range(HPB):
                            dve.wait_ge(*step_drained(l, m + 2 * TILES + h))
                            dve.tensor_reduce(neg_max[:, TILES * h:TILES * h + 1], probs[:, h, 0:P], AX_X,
                                              ALU.max, negate=True)
                            last = dve.tensor_reduce(neg_max[:, TILES * h + 1:TILES * h + 2],
                                                     probs[:, h, P:3 * P], AX_X, ALU.max, negate=True)
                        last.then_inc(neg_max_ready, 1)
                elif what == "sums":
                    dve.wait_ge(exp_ready, l * (HPB * GROUPS) + HPB * (g + 1))
                    dve.reciprocal(row_inv, row_sum).then_inc(inv_ready, 1)
                elif what == "values" and mixer == "attention":
                    s0 = m + STEPS[mixer] - TILES - HPB // 2
                    dve.wait_ge(inv_ready, l * GROUPS + (g + 1))
                    dve.wait_ge(*moved_out(l, n0 + 3))
                    for i in range(HPB // 2):
                        dve.wait_ge(*step_ready(l, s0 + i))
                        for hh in range(2):
                            for t in range(TILES):
                                h = 2 * i + hh
                                last = dve.scalar_tensor_tensor(
                                    z_sb[:, t, head(h)], side(s0 + i)[:, head(2 * hh + t)],
                                    row_inv[:, TILES * h + t:TILES * h + t + 1], z_sb[:, t, head(h)],
                                    ALU.mult, ALU.mult)
                        last.then_inc(drained[(s0 + i) % SIDE_BANKS], 1)
                elif what == "values":
                    s0 = m + STEPS[mixer] - TILES - HPB // 2
                    for i in range(HPB // 2):
                        h = HPB * g + 2 * i
                        gq = gamma_q[:, h:h + 2, :].unsqueeze(3).to_broadcast((P, 2, TILES, P))
                        dve.wait_ge(*step_ready(l, s0 + i))
                        dve.tensor_tensor(ret_o[:, 2 * i:2 * i + 2, :, :],
                                          side(s0 + i)[:, :].rearrange("p (h t e) -> p h t e", h=2, t=TILES), gq,
                                          ALU.mult).then_inc(drained[(s0 + i) % SIDE_BANKS], 1)
                elif what == "norm":
                    dve.wait_ge(o_squared, l * GROUPS + (g + 1))
                    dve.tensor_reduce(o_ssq, q_sb[:, :, :].rearrange("p a (b e) -> p (a b) e", e=P), AX_X,
                                      ALU.add).then_inc(o_ssq_ready, 1)
                elif what == "gate" and mixer == "retention":
                    dve.wait_ge(o_rstd_ready, l * GROUPS + (g + 1))
                    dve.wait_ge(*moved_out(l, n0 + 3))
                    for h in range(HPB):
                        for t in range(TILES):
                            last = dve.scalar_tensor_tensor(
                                z_sb[:, t, head(h)], ret_o[:, h, t, :],
                                o_rstd[:, TILES * h + t:TILES * h + t + 1], z_sb[:, t, head(h)],
                                ALU.mult, ALU.mult)
                    last.then_inc(ret_gated, 1)
                elif what == "gate":
                    dve.wait_ge(*moved_out(l, n0 + 2))
                    dve.wait_ge(*moved_out(l, n0 + 3))
                    for t in range(TILES):
                        dve.tensor_tensor(z_sb[:, t, :], z_sb[:, t, :], k_sb[:, t, :],
                                          ALU.mult).then_inc(conv_gated, 1)
                elif what in ("conv0", "conv1", "conv2"):
                    i = int(what[-1])
                    if i == 0:
                        for t in range(TILES):
                            dve.wait_ge(*step_drained(l, m + t))
                        dve.wait_ge(params_in, l * 32 + 32)
                    for c in range(HPB):
                        ch = HPB * g + c
                        src = prodT[:, c, 2 - i:2 - i + SEQ]
                        w = tap[2 - i][:, ch:ch + 1]
                        if i == 0:
                            dve.tensor_scalar(kT[:, c, :], src, w, conv_bias[:, ch:ch + 1], ALU.mult,
                                              ALU.add).then_inc(conv_steps, 1)
                        else:
                            dve.wait_ge(conv_steps, l * (3 * HPB * GROUPS) + (HPB * (3 * g + i - 1) + c + 1))
                            dve.scalar_tensor_tensor(kT[:, c, :], src, w, kT[:, c, :], ALU.mult,
                                                     ALU.add).then_inc(conv_steps, 1)
                elif what == "out":
                    s0 = m + STEPS[mixer] - TILES
                    for t in range(TILES):
                        s = s0 + t
                        if mixer == "conv":
                            dve.wait_ge(*step_ready(l, s))
                            if t == 0:
                                dve.wait_ge(conv_steps, l * (3 * HPB * GROUPS) + 3 * HPB * (g + 1))
                            dve.tensor_tensor(heads4(work2[:, t, :]), heads4(side(s)[:, :]), kT[:, :, tok(t)],
                                              ALU.mult).then_inc(drained[s % SIDE_BANKS], 1)
                    for t in range(TILES):
                        lead = oT_lead[:, HPB * g:HPB * (g + 1), tok(t)]
                        dst = oT_trail[:, HPB * g:HPB * (g + 1), tok(t)]
                        if mixer == "conv":
                            dve.wait_ge(*lead_steps(l, lead_no(mixer, g, t)))
                            dve.tensor_tensor(dst, heads4(work2[:, t, :]), lead.bitcast(F32),
                                              ALU.subtract).then_inc(conv_trail, 1)
                        else:
                            trail_of_step(l, s0 + t, lead_no(mixer, g, t), lead, dst)

            def x_trail_of(l, m):
                t, c = divmod(m, KT // HPB)
                dve.wait_ge(x_lead, l * X_STEPS + (m + 1))
                dve.tensor_tensor(hT_trail[:, HPB * c:HPB * (c + 1), tok(t)], heads4(work2[:, m % 2, :]),
                                  hT_lead[:, HPB * c:HPB * (c + 1), tok(t)].bitcast(F32),
                                  ALU.subtract).then_inc(x_trail, 1)

            dve.sem_inc(trail_ready, 2 * RAW_SLOTS)
            dve.sem_inc(half_done, SPLIT_SLOTS)
            for e in evicted:
                dve.sem_inc(e, TILES)
            for d in drained:
                dve.sem_inc(d, 1)
            dve.wait_ge(loads_in, 32)
            dve.wait_ge(zeroed, 2)
            dve.sem_inc(x_new, TILES)
            with dve.Fori(0, DEPTH) as l:
                dve.wait_ge(x_rstd_ready, l + 1)
                for t in range(TILES):
                    dve.tensor_scalar(merged[:, t, :], gates[:, t, :], x_rstd[:, t:t + 1], None,
                                      ALU.mult).then_inc(xn_ready, 1)
                dve.wait_ge(params_in, l * 32 + 32)
                for m in range(X_STEPS):
                    t, c = divmod(m, KT // HPB)
                    if m >= 2:
                        dve.wait_ge(x_trail, l * X_STEPS + (m - 1))
                    dve.wait_ge(*step_ready(l, m))
                    gain = pre_gain[:, HPB * c:HPB * (c + 1)].unsqueeze(2).to_broadcast((P, HPB, P))
                    dve.tensor_tensor(heads4(work2[:, m % 2, :]), heads4(side(m)[:, :]), gain,
                                      ALU.mult).then_inc(drained[m % SIDE_BANKS], 1)
                    if m >= 1:
                        x_trail_of(l, m - 1)
                x_trail_of(l, X_STEPS - 1)
                for h in range(HALVES + AHEAD):
                    if h < HALVES:
                        split_trail(l, h)
                    if h in EVICT_DUE:
                        evict(l, EVICT_DUE[h])
                    for what, mixer, g in DVE_DUE.get(h, []):
                        side_work(l, what, mixer, g)
                    if h in MERGE_DRAIN_DUE:
                        j = MERGE_DRAIN_DUE[h]
                        for t in range(TILES):
                            trail_of_step(l, MERGE_STEP0 + TILES * j + t, merge_lead_no(j, t),
                                          hT_lead[:, HPB * j:HPB * (j + 1), tok(t)],
                                          hT_trail[:, HPB * j:HPB * (j + 1), tok(t)])
                dve.tensor_reduce(y_sum, y_ssq.rearrange("p (t j) -> p t j", t=TILES), AX_X,
                                  ALU.add).then_inc(y_sum_ready, 1)
                dve.wait_ge(residual_in, l * 16 + 16)
                dve.wait_ge(y_rstd_ready, l + 1)
                for t in range(TILES):
                    dve.scalar_tensor_tensor(gates[:, t, :], merged[:, t, :], y_rstd[:, t:t + 1],
                                             gates[:, t, :], ALU.mult, ALU.add).then_inc(x_new, 1)


def constants():
    tq, tk = np.arange(SEQ)[:, None], np.arange(SEQ)[None, :]
    held = np.zeros((SEQ, SEQ))
    for window, dil in DILATIONS:
        held += (tq >= tk) & ((tq - tk) % dil == 0) & (tq - tk <= window)
    log_count = np.where(held > 0, np.log(np.maximum(held, 1.0)), -1e30)
    causal = (tk >= tq).astype(np.float64)
    parts = {
        "ident": np.eye(P),
        "log_count": np.concatenate([log_count[:P, :P], log_count[P:, :]], 1),
        "causal": np.concatenate([causal[:P, :], causal[P:, P:]], 1),
    }
    half = P // 2
    freq = (np.float32(ROPE_BASE) ** (-np.arange(half, dtype=np.float32) / np.float32(half))).astype(np.float32)
    angle = (np.arange(SEQ, dtype=np.float32)[:, None] * freq[None, :]).astype(np.float64)
    by_tile = lambda a: a.reshape(TILES, P, -1).transpose(1, 0, 2).reshape(P, -1)
    parts["cos"], parts["sin"] = by_tile(np.cos(angle)), by_tile(np.sin(angle))
    parts["neg_sin"] = -parts["sin"]
    log_gamma = np.log1p(-np.exp2(-5.0 - np.arange(HEADS)))
    decay = np.arange(SEQ).reshape(TILES, P).T[:, None, :] * log_gamma[None, :, None]
    parts["gamma_q"] = np.exp(decay).reshape(P, -1)
    parts["gamma_v"] = (np.exp(-decay) * P ** -0.5).reshape(P, -1)
    return np.concatenate([parts[n] for n, _ in CONST_PARTS], 1).astype(np.float32)


def kernel(x, pre_norm_g, post_norm_g, w_in, conv_w, conv_b, w_branch_a, w_branch_c, w_branch_r, w_out):
    import concourse.bacc as bacc
    from concourse.bass_utils import run_bass_kernel_spmd

    def by_channel(a):
        a = np.asarray(a)
        return a.reshape(DEPTH, -1, P).transpose(2, 0, 1)

    params = np.concatenate([by_channel(pre_norm_g), by_channel(conv_w), by_channel(conv_b)], 2)
    arrays = {
        "x": np.asarray(x).reshape(SEQ, D_MODEL),
        "w_in": w_in, "w_branch_a": w_branch_a, "w_branch_c": w_branch_c, "w_branch_r": w_branch_r,
        "w_out": w_out, "post_norm_g": post_norm_g,
        "params": params.reshape(P, DEPTH * PARAM_COLS),
        "constants": constants(),
    }
    arrays = {k: np.ascontiguousarray(v) for k, v in arrays.items()}
    nc = bacc.Bacc("TRN2", target_bir_lowering=False, num_devices=1)
    aps = [nc.dram_tensor(k, v.shape, mybir.dt.from_np(v.dtype), kind="ExternalInput").ap()
           for k, v in arrays.items()]
    out = nc.dram_tensor("out", (SEQ, D_MODEL), F32, kind="ExternalOutput").ap()
    build(nc, *aps, out)
    result = run_bass_kernel_spmd(nc, [arrays], core_ids=[0])
    return result.results[0]["out"].reshape(1, SEQ, D_MODEL)
```

```python
import math
from contextlib import ExitStack

import numpy as np

import concourse.bass as bass
from concourse import mybir

F32 = mybir.dt.float32
F32R = mybir.dt.float32r
ALU = mybir.AluOpType
ACT = mybir.ActivationFunctionType
AX_X = mybir.AxisListType.X

P = 128
DEPTH = 2
D_MODEL = 2048
SEQ = 256
TILES = SEQ // P
WIDTH = 1536
HEADS = WIDTH // P
DILATIONS = ((128, 1), (512, 4), (2048, 16))
ROPE_BASE = 10000.0
EPS = 1e-6

COLS = 512
HPB = COLS // P
GROUPS = WIDTH // COLS
OUT_BLOCKS = D_MODEL // COLS
KT = D_MODEL // P
KT_MIX = WIDTH // P
CHUNK = 4
HALF = 2
RAW_SLOTS = 4
SPLIT_SLOTS = 4
SIDE_BANKS = 4
MIXERS = ("attention", "conv", "retention")

SECTION = {"attention": {"q": 0, "k": 1, "v": 2, "z": 3},
           "conv": {"u": 4, "b": 5, "c": 6, "z": 7},
           "retention": {"q": 8, "k": 9, "v": 10, "z": 11}}
ROLES = {"attention": "vqkz", "conv": "ucbz", "retention": "vqkz"}
GATES_AT = 12 * GROUPS

STEPS = {"attention": TILES + TILES + HPB + HPB + HPB // 2 + TILES,
         "conv": TILES + TILES,
         "retention": TILES + TILES + HPB + HPB // 2 + TILES}
X_STEPS = TILES * KT // HPB
MERGE_STEPS = TILES * OUT_BLOCKS

CONST_PARTS = (("ident", P), ("log_count", 3 * P), ("causal", 3 * P), ("cos", TILES * 64),
               ("sin", TILES * 64), ("neg_sin", TILES * 64), ("gamma_q", TILES * HEADS),
               ("gamma_v", TILES * HEADS))
CONST_AT, CONST_COLS = {}, 0
for _name, _n in CONST_PARTS:
    CONST_AT[_name] = (CONST_COLS, CONST_COLS + _n)
    CONST_COLS += _n
PARAM_COLS = KT + 4 * KT_MIX


def layer_blocks():
    blocks = []
    for b, mixer in enumerate(MIXERS):
        for g in range(GROUPS):
            for role in ROLES[mixer]:
                blocks.append(("w_in", COLS * (GROUPS * SECTION[mixer][role] + g), KT,
                               ("mix", mixer, role, g)))
        for j in range(OUT_BLOCKS):
            blocks.append(("w_in", COLS * (GATES_AT + OUT_BLOCKS * b + j), KT, ("gate", mixer, "", j)))
        for j in range(OUT_BLOCKS):
            blocks.append((mixer, COLS * j, KT_MIX, ("branch", mixer, "", j)))
    for j in range(OUT_BLOCKS):
        blocks.append(("w_out", COLS * j, KT, ("out", "", "", j)))
    return blocks


BLOCKS = layer_blocks()
NBLOCKS = len(BLOCKS)
FIRST_HALF = [0]
for _b in BLOCKS:
    FIRST_HALF.append(FIRST_HALF[-1] + _b[2] // HALF)
HALVES = FIRST_HALF[-1]
CHUNKS = HALVES * HALF // CHUNK
BLOCK_OF = [n for n, _b in enumerate(BLOCKS) for _ in range(_b[2] // HALF)]
PER_BLOCK_GROUP = len(ROLES["attention"])
MIXER_BLOCKS = PER_BLOCK_GROUP * GROUPS + 2 * OUT_BLOCKS

AHEAD = SPLIT_SLOTS
def split_before(j):
    return [0] if j == 0 else [2 * j - 1, 2 * j]


X_HALVES = 2 * OUT_BLOCKS - 1


def first_block(mixer, g):
    return MIXER_BLOCKS * MIXERS.index(mixer) + PER_BLOCK_GROUP * g


def step0(mixer, g):
    before = X_STEPS
    for m in MIXERS[:MIXERS.index(mixer)]:
        before += GROUPS * STEPS[m]
    return before + g * STEPS[mixer]


MERGE_STEP0 = step0("retention", GROUPS)
SIDE_STEPS = MERGE_STEP0 + MERGE_STEPS
assert NBLOCKS % 2 == 0 and SIDE_STEPS % SIDE_BANKS == 0
assert HALVES % SPLIT_SLOTS == 0 and CHUNKS % RAW_SLOTS == 0

B = KT // HALF


def due(table, offset=0):
    out = {}
    for mixer, whats in table.items():
        for g in range(GROUPS):
            for what, at in whats:
                out.setdefault(FIRST_HALF[first_block(mixer, g)] + at + offset, []).append((what, mixer, g))
    return out


PE_DUE = due({
    "attention": [("q", 2 * B + 3), ("k", 3 * B + 2), ("scores", 3 * B + 4), ("probs", 4 * B + 2),
                  ("values", 4 * B + 4), ("out", 4 * B + 6)],
    "conv": [("prod", 2 * B + 2), ("out", 4 * B + 2)],
    "retention": [("q", 2 * B + 3), ("k", 3 * B + 3), ("scores", 3 * B + 5), ("values", 4 * B + 1),
                  ("out", 4 * B + 6)]})
ACT_DUE = due({
    "attention": [("q", 2 * B + 3), ("k", 3 * B + 2), ("exp", 3 * B + 5), ("probs", 4 * B + 2),
                  ("out", 4 * B + 6)],
    "conv": [("prod", 2 * B + 2), ("out", 4 * B + 2)],
    "retention": [("q", 2 * B + 3), ("k", 3 * B + 3), ("square", 4 * B + 1), ("out", 4 * B + 6)]}, AHEAD)
DVE_DUE = due({
    "attention": [("scores", 3 * B + 4), ("sums", 4 * B + 1), ("values", 4 * B + 4), ("out", 4 * B + 6)],
    "conv": [("conv0", 2 * B + 3), ("conv1", 2 * B + 4), ("conv2", 2 * B + 5), ("gate", 4 * B),
             ("out", 4 * B + 2)],
    "retention": [("scores", 3 * B + 5), ("values", 4 * B + 1), ("norm", 4 * B + 2),
                  ("gate", 4 * B + 3), ("out", 4 * B + 6)]}, AHEAD)
EVICT_DUE = {FIRST_HALF[n + 1] - 1 + AHEAD: n for n in range(NBLOCKS)}
SQUARES_FROM = B
EVICT_DUE[SQUARES_FROM + OUT_BLOCKS + 2] = EVICT_DUE.pop(FIRST_HALF[1] - 1 + AHEAD)
MERGE_BLOCK0 = first_block("retention", GROUPS) + OUT_BLOCKS
MERGE_DUE = {FIRST_HALF[MERGE_BLOCK0 + j + 1] + 2: j for j in range(OUT_BLOCKS)}
MERGE_DRAIN_DUE = {h + AHEAD: j for h, j in MERGE_DUE.items()}
RESIDUAL_DUE = FIRST_HALF[MERGE_BLOCK0 + OUT_BLOCKS] + AHEAD + 1


def build(nc, x, w_in, w_attention, w_conv, w_retention, w_out, post_g, params, consts, out):
    weights = {
        "w_in": w_in.rearrange("l (k p) n -> p (l k) n", p=P),
        "attention": w_attention.rearrange("l (k p) n -> p (l k) n", p=P),
        "conv": w_conv.rearrange("l (k p) n -> p (l k) n", p=P),
        "retention": w_retention.rearrange("l (k p) n -> p (l k) n", p=P),
        "w_out": w_out.rearrange("l (k p) n -> p (l k) n", p=P),
    }
    x_rows = x.rearrange("(t p) d -> p t d", p=P)
    out_rows = out.rearrange("(t p) d -> p t d", p=P)

    with ExitStack() as ctx:
        def sb(name, shape, dt=F32):
            return ctx.enter_context(nc.sbuf_tensor(name, shape, dt))

        def sem(name):
            return ctx.enter_context(nc.semaphore(name))

        raw = sb("raw", [P, RAW_SLOTS, CHUNK * COLS])
        w_lead = sb("w_lead", [P, SPLIT_SLOTS, HALF * COLS], F32R)
        w_trail = sb("w_trail", [P, SPLIT_SLOTS, HALF * COLS], F32R)
        hT_lead = sb("hT_lead", [P, KT, SEQ], F32R)
        hT_trail = sb("hT_trail", [P, KT, SEQ], F32R)
        oT_lead = sb("oT_lead", [P, KT_MIX, SEQ], F32R)
        oT_trail = sb("oT_trail", [P, KT_MIX, SEQ], F32R)
        merged = sb("merged", [P, TILES, D_MODEL])
        gates = sb("gates", [P, TILES, D_MODEL])
        post_gain = sb("post_gain", [P, D_MODEL])
        v_sb = sb("v_sb", [P, TILES, COLS])
        q_sb = sb("q_sb", [P, TILES, COLS])
        k_sb = sb("k_sb", [P, TILES, COLS])
        z_sb = sb("z_sb", [P, TILES, COLS])
        qT = sb("qT", [P, HPB, SEQ])
        kT = sb("kT", [P, HPB, SEQ])
        prodT = sb("prodT", [P, HPB, 2 + SEQ])
        probs = sb("probs", [P, HPB, 3 * P])
        probsT = sb("probsT", [P, HPB, 3 * P])
        par_all = sb("par_all", [P, DEPTH * PARAM_COLS])
        par = sb("par", [P, PARAM_COLS])
        cst = sb("cst", [P, CONST_COLS])
        stat = sb("stat", [P, 72])
        exponent = sb("exponent", [P, 8])

        ps = [ctx.enter_context(nc.psum_tensor(f"ps{i}", [P, COLS], F32)) for i in range(8)]

        def const(name):
            a, b = CONST_AT[name]
            return cst[:, a:b]

        ident = const("ident")
        gamma_q = const("gamma_q").rearrange("p (h t) -> p h t", t=TILES)
        gamma_v = const("gamma_v").rearrange("p (h t) -> p h t", t=TILES)
        rope = {n: const(n).rearrange("p (t f) -> p t f", t=TILES) for n in ("cos", "sin", "neg_sin")}
        pre_gain = par[:, 0:KT]
        tap = [par[:, KT + i * KT_MIX:KT + (i + 1) * KT_MIX] for i in range(3)]
        conv_bias = par[:, KT + 3 * KT_MIX:KT + 4 * KT_MIX]

        x_ssq, x_sum, x_rstd = stat[:, 56:64], stat[:, 0:2], stat[:, 2:4]
        y_ssq, y_sum, y_rstd = stat[:, 4:12], stat[:, 12:14], stat[:, 14:16]
        neg_max, row_sum, row_inv = stat[:, 16:24], stat[:, 24:32], stat[:, 32:40]
        o_ssq, o_rstd = stat[:, 40:48], stat[:, 48:56]

        work = probs[:, :, :].rearrange("p h c -> p (h c)")
        work2 = work[:, 0:2 * COLS].rearrange("p (s c) -> p s c", s=2)
        ret_o = work[:, 0:HPB * TILES * P].rearrange("p (h t e) -> p h t e", h=HPB, t=TILES)

        raw_in = [sem(f"raw_in{i}") for i in range(RAW_SLOTS)]
        lead_ready = sem("lead_ready")
        trail_ready = sem("trail_ready")
        half_done = sem("half_done")
        evicted = [sem(f"evicted{i}") for i in range(2)]
        side_ready = sem("side_ready")
        drained = [sem(f"drained{i}") for i in range(SIDE_BANKS)]
        ident_in = sem("ident_in")
        params_in = sem("params_in")
        tables_in = sem("tables_in")
        residual_in = [sem(f"residual_in{j}") for j in range(OUT_BLOCKS)]
        zeroed = sem("zeroed")
        par_ready = sem("par_ready")
        post_gain_in = sem("post_gain_in")
        x_new = sem("x_new")
        x_squared = sem("x_squared")
        x_sum_ready = sem("x_sum_ready")
        x_mean = sem("x_mean")
        x_rstd_ready = sem("x_rstd_ready")
        x_lead = sem("x_lead")
        sig_ready = sem("sig_ready")
        rotated = sem("rotated")
        maxes = sem("maxes")
        neg_max_ready = sem("neg_max_ready")
        exp_ready = sem("exp_ready")
        inv_ready = sem("inv_ready")
        conv_steps = sem("conv_steps")
        conv_gated = sem("conv_gated")
        conv_trail = sem("conv_trail")
        o_squared = sem("o_squared")
        o_ssq_ready = sem("o_ssq_ready")
        o_mean = sem("o_mean")
        o_rstd_ready = sem("o_rstd_ready")
        ret_gated = sem("ret_gated")
        out_lead = sem("out_lead")
        merged_ready = sem("merged_ready")
        y_squared = sem("y_squared")
        y_sum_ready = sem("y_sum_ready")
        y_mean = sem("y_mean")
        y_rstd_ready = sem("y_rstd_ready")
        residual_out = sem("residual_out")
        output_out = sem("output_out")
        sp_passed = sem("sp_passed")
        pool_passed = sem("pool_passed")

        def chunk_landed(l, i):
            return raw_in[i % RAW_SLOTS], l * (16 * CHUNKS // RAW_SLOTS) + 16 * (i // RAW_SLOTS + 1)

        def done_half(l, h):
            return half_done, l * HALVES + (SPLIT_SLOTS + h + 1)

        def done_block(l, n):
            return done_half(l, FIRST_HALF[n + 1] - 1)

        def moved_out(l, n):
            return evicted[n % 2], l * (TILES * NBLOCKS // 2) + TILES * (n // 2 + 2)

        def bank_free(l, n):
            return evicted[n % 2], l * (TILES * NBLOCKS // 2) + TILES * (n // 2 + 1)

        def step_ready(l, m):
            return side_ready, l * SIDE_STEPS + (m + 1)

        def step_drained(l, m):
            return drained[m % SIDE_BANKS], l * (SIDE_STEPS // SIDE_BANKS) + (m // SIDE_BANKS + 2)

        def side_bank_free(l, m):
            return drained[m % SIDE_BANKS], l * (SIDE_STEPS // SIDE_BANKS) + (m // SIDE_BANKS + 1)

        def count(semaphore, per_layer):
            return lambda l, n: (semaphore, l * per_layer + n)

        group_no = {(m, g): GROUPS * i + g for i, m in enumerate(MIXERS) for g in range(GROUPS)}
        sig_tiles = count(sig_ready, TILES * 3 * GROUPS)
        rotated_tiles = count(rotated, 2 * TILES * GROUPS)
        lead_steps = count(out_lead, TILES * 3 * GROUPS + MERGE_STEPS)
        merged_tiles = count(merged_ready, 2 * TILES * OUT_BLOCKS)

        def lead_no(mixer, g, t):
            return TILES * group_no[mixer, g] + t + 1

        def merge_lead_no(j, t):
            return TILES * 3 * GROUPS + TILES * j + t + 1

        def bank(n, t):
            return ps[2 * (n % 2) + t]

        def side(m):
            return ps[4 + m % SIDE_BANKS]

        def tok(t):
            return slice(t * P, (t + 1) * P)

        def head(h):
            return slice(h * P, (h + 1) * P)

        def heads4(ap):
            return ap.rearrange("p (h c) -> p h c", h=HPB)

        block = ctx.enter_context(nc.Block())

        @block.sync
        def _(sp):
            sp.dma_start(ident, consts[:, 0:P]).then_inc(ident_in, 16)
            sp.dma_start(par_all[:, :], params).then_inc(params_in, 16)
            sp.dma_start(gates[:, :, 0:COLS], x_rows[:, :, 0:COLS]).then_inc(residual_in[0], 16)
            with sp.Fori(0, DEPTH) as l:
                for n, (name, col, tiles, _what) in enumerate(BLOCKS):
                    for c in range(tiles // CHUNK):
                        i = FIRST_HALF[n] * HALF // CHUNK + c
                        sp.wait_ge(trail_ready, l * HALVES + (2 * i + 2))
                        sp.sem_inc(sp_passed, 1)
                        sp.dma_start(
                            raw[:, i % RAW_SLOTS, :].rearrange("p (k n) -> p k n", k=CHUNK),
                            weights[name][:, bass.ds(l * tiles + c * CHUNK, CHUNK), col:col + COLS],
                        ).then_inc(raw_in[i % RAW_SLOTS], 16)
            for j in range(OUT_BLOCKS):
                cols = slice(COLS * j, COLS * (j + 1))
                sp.wait_ge(x_new, DEPTH * X_STEPS + TILES * (j + 1))
                sp.dma_start(out_rows[:, :, cols], gates[:, :, cols]).then_inc(output_out, 16)
            sp.wait_ge(output_out, 16 * OUT_BLOCKS)

        @block.gpsimd
        def _(pool):
            def wait(semaphore, value):
                pool.wait_ge(semaphore, value)
                pool.sem_inc(pool_passed, 1)

            def rstd(src, mean_sem, mean_value, dst, width, n):
                pool.tensor_scalar(dst, src, 1.0 / width, EPS, ALU.mult, ALU.add).then_inc(mean_sem, 1)
                pool.wait_ge(mean_sem, mean_value)
                return pool.tensor_tensor(dst, dst, exponent[:, 0:n], ALU.pow)

            pool.memset(exponent[:, :], -0.5).then_inc(zeroed, 1)
            pool.memset(prodT[:, :, 0:2], 0.0).then_inc(zeroed, 1)
            pool.wait_ge(zeroed, 2)
            pool.wait_ge(half_done, SPLIT_SLOTS + 2)
            pool.dma_start(cst[:, P:], consts[:, P:]).then_inc(tables_in, 16)

            with pool.Fori(0, DEPTH) as l:
                for j in range(OUT_BLOCKS):
                    cols = slice(COLS * j, COLS * (j + 1))
                    wait(x_new, l * X_STEPS + TILES * (j + 1))
                    pool.dma_start(out_rows[:, :, cols], gates[:, :, cols]).then_inc(residual_out, 16)
                wait(x_sum_ready, l + 1)
                rstd(x_sum, x_mean, l + 1, x_rstd, D_MODEL, 2).then_inc(x_rstd_ready, 1)
                pool.dma_start(post_gain[:, :], post_g[bass.ds(l, 1), :].to_broadcast((P, D_MODEL))).then_inc(post_gain_in, 16)
                for g in range(GROUPS):
                    wait(o_ssq_ready, l * GROUPS + (g + 1))
                    rstd(o_ssq, o_mean, l * GROUPS + (g + 1), o_rstd, P, 8).then_inc(o_rstd_ready, 1)
                wait(y_sum_ready, l + 1)
                rstd(y_sum, y_mean, l + 1, y_rstd, D_MODEL, 2).then_inc(y_rstd_ready, 1)
            pool.wait_ge(residual_out, 16 * OUT_BLOCKS * DEPTH)

        @block.tensor
        def _(pe):
            def transposes(l, m, sources):
                pe.wait_ge(*side_bank_free(l, m))
                for i, s in enumerate(sources):
                    last = pe.transpose(side(m)[:, head(i)], s, ident)
                last.then_inc(side_ready, 1)

            def side_steps(l, what, mixer, g):
                m = step0(mixer, g)
                n0 = first_block(mixer, g)
                if what in ("q", "k"):
                    i = "qk".index(what)
                    if mixer == "attention":
                        pe.wait_ge(*moved_out(l, n0 + 1 + i))
                    else:
                        pe.wait_ge(*rotated_tiles(l, TILES * (2 * g + i + 1)))
                    src = (q_sb, k_sb)[i]
                    for t in range(TILES):
                        transposes(l, m + TILES * i + t, [src[:, t, head(h)] for h in range(HPB)])
                elif what == "prod":
                    pe.wait_ge(*moved_out(l, n0 + 1))
                    for t in range(TILES):
                        transposes(l, m + t, [q_sb[:, t, head(h)] for h in range(HPB)])
                elif what == "scores":
                    for i in range(2 * TILES):
                        pe.wait_ge(*step_drained(l, m + i))
                    for h in range(HPB):
                        s = m + 2 * TILES + h
                        pe.wait_ge(*side_bank_free(l, s))
                        if mixer == "attention":
                            pe.matmul(side(s)[:, 0:P], qT[:, h, 0:P], kT[:, h, 0:P], start=True, stop=True)
                            pe.matmul(side(s)[:, P:3 * P], qT[:, h, P:SEQ], kT[:, h, :],
                                      start=True, stop=True).then_inc(side_ready, 1)
                        else:
                            pe.matmul(side(s)[:, 0:SEQ], kT[:, h, 0:P], qT[:, h, :], start=True, stop=True)
                            pe.matmul(side(s)[:, SEQ:3 * P], kT[:, h, P:SEQ], qT[:, h, P:SEQ],
                                      start=True, stop=True).then_inc(side_ready, 1)
                elif what == "probs":
                    for h in range(HPB):
                        s = m + 2 * TILES + HPB + h
                        pe.wait_ge(exp_ready, l * (HPB * GROUPS) + (HPB * g + h + 1))
                        pe.wait_ge(*side_bank_free(l, s))
                        for i in range(3):
                            last = pe.transpose(side(s)[:, head(i)], probs[:, h, head(i)], ident)
                        last.then_inc(side_ready, 1)
                elif what == "values":
                    pe.wait_ge(*moved_out(l, n0))
                    s0 = m + STEPS[mixer] - TILES - HPB // 2
                    for i in range(HPB):
                        pe.wait_ge(*step_drained(l, s0 - HPB + i))
                    for i in range(HPB // 2):
                        pe.wait_ge(*side_bank_free(l, s0 + i))
                        for hh in range(2):
                            h = 2 * i + hh
                            o = side(s0 + i)[:, 2 * hh * P:(2 * hh + 2) * P]
                            pe.matmul(o[:, 0:P], probsT[:, h, 0:P], v_sb[:, 0, head(h)], start=True, stop=True)
                            pe.matmul(o[:, P:2 * P], probsT[:, h, P:2 * P], v_sb[:, 0, head(h)],
                                      start=True, stop=False)
                            last = pe.matmul(o[:, P:2 * P], probsT[:, h, 2 * P:3 * P], v_sb[:, 1, head(h)],
                                             start=False, stop=True)
                        last.then_inc(side_ready, 1)
                elif what == "out":
                    s0 = m + STEPS[mixer] - TILES
                    if mixer == "attention":
                        for i in range(HPB // 2):
                            pe.wait_ge(*step_drained(l, s0 - HPB // 2 + i))
                    elif mixer == "conv":
                        pe.wait_ge(conv_gated, l * (TILES * GROUPS) + TILES * (g + 1))
                    else:
                        pe.wait_ge(ret_gated, l * GROUPS + (g + 1))
                    for t in range(TILES):
                        transposes(l, s0 + t, [z_sb[:, t, head(h)] for h in range(HPB)])

            def wait_stationary(l, n, k):
                kind, mixer, _role, j = BLOCKS[n][3]
                if n == 0 and k % HPB == 0:
                    for t in range(TILES):
                        pe.wait_ge(*step_drained(l, TILES * (k // HPB) + t))
                elif kind == "branch" and j == 0 and k == 0:
                    if mixer == "conv":
                        pe.wait_ge(conv_trail, l * (TILES * GROUPS) + TILES * GROUPS)
                    else:
                        s = step0(mixer, GROUPS - 1) + STEPS[mixer] - TILES
                        for t in range(TILES):
                            pe.wait_ge(*step_drained(l, s + t))
                elif kind == "out" and j == 0 and k % HPB == 0:
                    for t in range(TILES):
                        pe.wait_ge(*step_drained(l, MERGE_STEP0 + TILES * (k // HPB) + t))

            def multiply(l, h):
                n = BLOCK_OF[h]
                kind = BLOCKS[n][3][0]
                lead, trail = (oT_lead, oT_trail) if kind == "branch" else (hT_lead, hT_trail)
                slot = h % SPLIT_SLOTS
                k0 = HALF * (h - FIRST_HALF[n])
                wait_stationary(l, n, k0)
                if k0 == 0:
                    pe.wait_ge(*bank_free(l, n))
                pe.wait_ge(trail_ready, l * HALVES + (2 * RAW_SLOTS + h + 1))
                for i in range(HALF):
                    if i == 1 and h % 2 == 0 and h // 2 + 1 < OUT_BLOCKS:
                        x_steps(l, TILES * (h // 2 + 1), TILES * (h // 2 + 2))
                    k = k0 + i
                    wl = w_lead[:, slot, i * COLS:(i + 1) * COLS]
                    wt = w_trail[:, slot, i * COLS:(i + 1) * COLS]
                    for t in range(TILES):
                        acc = bank(n, t)[:, :]
                        pe.matmul(acc, lead[:, k, tok(t)], wl, start=(k == 0), stop=False)
                        pe.matmul(acc, lead[:, k, tok(t)], wt, start=False, stop=False)
                        last = pe.matmul(acc, trail[:, k, tok(t)], wl, start=False,
                                         stop=(k == BLOCKS[n][2] - 1))
                last.then_inc(half_done, 1)

            def x_steps(l, first, last):
                for m in range(first, last):
                    j, t = divmod(m, TILES)
                    pe.wait_ge(x_new, l * X_STEPS + (m + 1))
                    transposes(l, m, [gates[:, t, head(HPB * j + i)] for i in range(HPB)])

            pe.wait_ge(ident_in, 16)
            with pe.Fori(0, DEPTH) as l:
                x_steps(l, 0, TILES)
                for h in range(HALVES):
                    multiply(l, h)
                    for what, mixer, g in PE_DUE.get(h, []):
                        side_steps(l, what, mixer, g)
                    if h in MERGE_DUE:
                        j = MERGE_DUE[h]
                        pe.wait_ge(*merged_tiles(l, TILES * (OUT_BLOCKS + j + 1)))
                        for t in range(TILES):
                            transposes(l, MERGE_STEP0 + TILES * j + t,
                                       [merged[:, t, head(HPB * j + i)] for i in range(HPB)])

        @block.scalar
        def _(act):
            def split_lead(l, h):
                i = h * HALF // CHUNK
                part = (h * HALF % CHUNK) * COLS
                if part == 0:
                    act.wait_ge(*chunk_landed(l, i))
                act.wait_ge(half_done, l * HALVES + (h + 1))
                act.activation(w_lead[:, h % SPLIT_SLOTS, :], raw[:, i % RAW_SLOTS, part:part + HALF * COLS],
                               ACT.Copy).then_inc(lead_ready, 1)

            def evict(l, n):
                kind, mixer, role, j = BLOCKS[n][3]
                if n == 0:
                    act.wait_ge(x_rstd_ready, l + 1)
                if kind == "mix":
                    copy_to = {("attention", "v"): v_sb, ("attention", "q"): q_sb, ("attention", "k"): k_sb,
                               ("conv", "u"): v_sb, ("conv", "b"): k_sb}.get((mixer, role))
                    if copy_to is not None:
                        act.wait_ge(*done_block(l, n))
                        for t in range(TILES):
                            act.activation(copy_to[:, t, :], bank(n, t)[:, :], ACT.Copy,
                                           scale=x_rstd[:, t:t + 1]).then_inc(evicted[n % 2], 1)
                    elif role == "z":
                        act.wait_ge(*done_block(l, n))
                        for t in range(TILES):
                            act.activation(z_sb[:, t, :], bank(n, t)[:, :], ACT.Sigmoid,
                                           scale=x_rstd[:, t:t + 1]).then_inc(sig_ready, 1)
                elif kind == "gate":
                    act.wait_ge(*done_block(l, n))
                    if mixer == MIXERS[0] and j == 0:
                        act.wait_ge(residual_out, l * (16 * OUT_BLOCKS) + 16 * OUT_BLOCKS)
                    for t in range(TILES):
                        act.activation(gates[:, t, COLS * j:COLS * (j + 1)], bank(n, t)[:, :],
                                       ACT.Sigmoid, scale=x_rstd[:, t:t + 1]).then_inc(evicted[n % 2], 1)
                elif kind == "out":
                    act.wait_ge(*done_block(l, n))
                    for t in range(TILES):
                        act.activation(z_sb[:, t, :], bank(n, t)[:, :], ACT.Square,
                                       accum_out=y_ssq[:, OUT_BLOCKS * t + j:OUT_BLOCKS * t + j + 1]).then_inc(y_squared, 1)

            def lead_of_step(l, s, dst):
                act.wait_ge(*step_ready(l, s))
                act.activation(dst, heads4(side(s)[:, :]), ACT.Copy).then_inc(out_lead, 1)

            def side_work(l, what, mixer, g):
                m = step0(mixer, g)
                if what in ("q", "k", "prod"):
                    i = 1 if what == "k" else 0
                    for t in range(TILES):
                        s = m + TILES * i + t
                        dst = prodT[:, :, 2 + t * P:2 + (t + 1) * P] if what == "prod" else (qT, kT)[i][:, :, tok(t)]
                        act.wait_ge(*step_ready(l, s))
                        act.activation(dst, heads4(side(s)[:, :]), ACT.Copy).then_inc(drained[s % SIDE_BANKS], 1)
                elif what == "exp":
                    act.wait_ge(neg_max_ready, l * GROUPS + (g + 1))
                    for h in range(HPB):
                        for t, cols in ((0, slice(0, P)), (1, slice(P, 3 * P))):
                            c = TILES * h + t
                            last = act.activation(probs[:, h, cols], probs[:, h, cols], ACT.Exp,
                                                  bias=neg_max[:, c:c + 1], accum_out=row_sum[:, c:c + 1])
                        last.then_inc(exp_ready, 1)
                elif what == "probs":
                    for h in range(HPB):
                        s = m + 2 * TILES + HPB + h
                        act.wait_ge(*step_ready(l, s))
                        act.activation(probsT[:, h, :], side(s)[:, 0:3 * P], ACT.Copy).then_inc(drained[s % SIDE_BANKS], 1)
                elif what == "square":
                    s0 = m + STEPS[mixer] - TILES - HPB // 2
                    for i in range(HPB // 2):
                        act.wait_ge(*step_drained(l, s0 + i))
                    act.activation(q_sb[:, :, :].rearrange("p a c -> p (a c)"),
                                   ret_o.rearrange("p h t e -> p (h t e)"), ACT.Square).then_inc(o_squared, 1)
                elif what == "out":
                    s0 = m + STEPS[mixer] - TILES
                    for t in range(TILES):
                        dst = oT_lead[:, HPB * g:HPB * (g + 1), tok(t)]
                        if mixer == "conv":
                            act.wait_ge(*step_drained(l, s0 + t))
                            act.activation(dst, heads4(work2[:, t, :]), ACT.Copy).then_inc(out_lead, 1)
                        else:
                            lead_of_step(l, s0 + t, dst)

            def x_lead_of(l, m):
                j, t = divmod(m, TILES)
                act.wait_ge(*step_ready(l, m))
                for i in range(HPB):
                    k = HPB * j + i
                    last = act.activation(hT_lead[:, k, tok(t)], side(m)[:, head(i)], ACT.Copy,
                                          scale=pre_gain[:, k:k + 1])
                last.then_inc(x_lead, 1)

            act.wait_ge(residual_in[0], 16)
            for j in range(1, OUT_BLOCKS):
                cols = slice(COLS * j, COLS * (j + 1))
                act.dma_start(gates[:, :, cols], x_rows[:, :, cols]).then_inc(residual_in[j], 16)
            act.wait_ge(params_in, 16)
            with act.Fori(0, DEPTH) as l:
                act.activation(par[:, :], par_all[:, bass.ds(l * PARAM_COLS, PARAM_COLS)],
                               ACT.Copy).then_inc(par_ready, 1)
                for j in range(OUT_BLOCKS):
                    for h in split_before(j):
                        split_lead(l, h)
                    if j == 0:
                        act.wait_ge(par_ready, l + 1)
                    for t in range(TILES):
                        x_lead_of(l, TILES * j + t)
                for h in range(X_HALVES, HALVES + AHEAD):
                    if h < HALVES:
                        split_lead(l, h)
                    if 0 <= h - SQUARES_FROM < OUT_BLOCKS:
                        j = h - SQUARES_FROM
                        cols = slice(COLS * j, COLS * (j + 1))
                        for t in range(TILES):
                            act.wait_ge(x_new, l * X_STEPS + X_STEPS)
                            c = OUT_BLOCKS * t + j
                            act.activation(merged[:, t, cols], gates[:, t, cols], ACT.Square,
                                           accum_out=x_ssq[:, c:c + 1]).then_inc(x_squared, 1)
                    if h in EVICT_DUE:
                        evict(l, EVICT_DUE[h])
                    for what, mixer, g in ACT_DUE.get(h, []):
                        side_work(l, what, mixer, g)
                    if h == RESIDUAL_DUE:
                        act.wait_ge(*merged_tiles(l, 2 * TILES * OUT_BLOCKS))
                        act.wait_ge(residual_out, l * (16 * OUT_BLOCKS) + 16 * OUT_BLOCKS)
                        for j in range(OUT_BLOCKS):
                            cols = slice(COLS * j, COLS * (j + 1))
                            act.dma_start(gates[:, :, cols], out_rows[:, :, cols]).then_inc(residual_in[j], 16)
                    if h in MERGE_DRAIN_DUE:
                        j = MERGE_DRAIN_DUE[h]
                        for t in range(TILES):
                            lead_of_step(l, MERGE_STEP0 + TILES * j + t, hT_lead[:, HPB * j:HPB * (j + 1), tok(t)])

        @block.vector
        def _(dve):
            def split_trail(l, h):
                i = h * HALF // CHUNK
                part = (h * HALF % CHUNK) * COLS
                s = h % SPLIT_SLOTS
                dve.wait_ge(lead_ready, l * HALVES + (h + 1))
                dve.tensor_tensor(w_trail[:, s, :], raw[:, i % RAW_SLOTS, part:part + HALF * COLS],
                                  w_lead[:, s, :].bitcast(F32), ALU.subtract).then_inc(trail_ready, 1)

            def rotate(l, n, g, role):
                dst = q_sb if role == "q" else k_sb
                dve.wait_ge(*done_block(l, n))
                for t in range(TILES):
                    src = bank(n, t)[:, :].rearrange("p (h s f) -> p h s f", h=HPB, s=2)
                    sin_part = work2[:, 1, :].rearrange("p (h s f) -> p h s f", h=HPB, s=2)
                    if t > 0:
                        dve.wait_ge(*rotated_tiles(l, TILES * (2 * g + "qk".index(role)) + t))
                    for s in range(2):
                        table = rope["neg_sin" if s == 0 else "sin"][:, t, :]
                        dve.scalar_tensor_tensor(sin_part[:, :, s, :], src[:, :, 1 - s, :], x_rstd[:, t:t + 1],
                                                 table.unsqueeze(1).to_broadcast((P, HPB, 64)),
                                                 ALU.mult, ALU.mult)
                    cos = rope["cos"][:, t, :].unsqueeze(1).to_broadcast((P, 2 * HPB, 64))
                    dve.scalar_tensor_tensor(
                        work2[:, 0, :].rearrange("p (h f) -> p h f", f=64),
                        bank(n, t)[:, :].rearrange("p (h f) -> p h f", f=64), x_rstd[:, t:t + 1], cos,
                        ALU.mult, ALU.mult).then_inc(evicted[n % 2], 1)
                    dve.wait_ge(evicted[n % 2], l * (TILES * NBLOCKS // 2) + (TILES * (n // 2 + 1) + t + 1))
                    dve.tensor_tensor(dst[:, t, :], work2[:, 0, :], work2[:, 1, :], ALU.add).then_inc(rotated, 1)

            def evict(l, n):
                kind, mixer, role, j = BLOCKS[n][3]
                if n == 0:
                    dve.wait_ge(x_rstd_ready, l + 1)
                    dve.wait_ge(tables_in, 16)
                if kind == "mix" and role == "z":
                    for t in range(TILES):
                        dve.wait_ge(*sig_tiles(l, TILES * group_no[mixer, j] + t + 1))
                        dve.scalar_tensor_tensor(z_sb[:, t, :], bank(n, t)[:, :], x_rstd[:, t:t + 1],
                                                 z_sb[:, t, :], ALU.mult, ALU.mult).then_inc(evicted[n % 2], 1)
                elif kind == "mix" and mixer == "retention" and role in "qk":
                    rotate(l, n, j, role)
                elif kind == "mix" and mixer == "retention":
                    dve.wait_ge(*done_block(l, n))
                    for t in range(TILES):
                        gv = gamma_v[:, HPB * j:HPB * (j + 1), t].unsqueeze(2).to_broadcast((P, HPB, P))
                        dve.scalar_tensor_tensor(heads4(v_sb[:, t, :]), heads4(bank(n, t)[:, :]),
                                                 x_rstd[:, t:t + 1], gv, ALU.mult, ALU.mult).then_inc(evicted[n % 2], 1)
                elif kind == "mix" and role == "c":
                    dve.wait_ge(*moved_out(l, n - 1))
                    dve.wait_ge(*done_block(l, n))
                    for t in range(TILES):
                        dve.scalar_tensor_tensor(q_sb[:, t, :], bank(n, t)[:, :], x_rstd[:, t:t + 1],
                                                 v_sb[:, t, :], ALU.mult, ALU.mult).then_inc(evicted[n % 2], 1)
                elif kind == "branch":
                    b = MIXERS.index(mixer)
                    cols = slice(COLS * j, COLS * (j + 1))
                    dve.wait_ge(*moved_out(l, n - OUT_BLOCKS))
                    dve.wait_ge(*done_block(l, n))
                    for t in range(TILES):
                        dst = merged if b == 0 else gates
                        dve.tensor_tensor(dst[:, t, cols], bank(n, t)[:, :], gates[:, t, cols],
                                          ALU.mult).then_inc(evicted[n % 2], 1)
                    if b > 0:
                        dve.wait_ge(*moved_out(l, n))
                        for t in range(TILES):
                            dve.tensor_tensor(merged[:, t, cols], merged[:, t, cols], gates[:, t, cols],
                                              ALU.add).then_inc(merged_ready, 1)
                elif kind == "out":
                    if j == 0:
                        dve.wait_ge(*step_ready(l, MERGE_STEP0 + MERGE_STEPS - 1))
                        dve.wait_ge(post_gain_in, l * 16 + 16)
                    for t in range(TILES):
                        dve.wait_ge(y_squared, l * (TILES * OUT_BLOCKS) + (TILES * j + t + 1))
                        if j == OUT_BLOCKS - 1 and t == TILES - 1:
                            dve.tensor_reduce(y_sum, y_ssq.rearrange("p (t j) -> p t j", t=TILES), AX_X,
                                              ALU.add).then_inc(y_sum_ready, 1)
                        dve.tensor_tensor(merged[:, t, COLS * j:COLS * (j + 1)], bank(n, t)[:, :],
                                          post_gain[:, COLS * j:COLS * (j + 1)], ALU.mult).then_inc(evicted[n % 2], 1)
                    if j == OUT_BLOCKS - 1:
                        dve.wait_ge(*moved_out(l, n))

            def trail_of_step(l, s, lead_count, lead, dst):
                dve.wait_ge(*lead_steps(l, lead_count))
                dve.tensor_tensor(dst, heads4(side(s)[:, :]), lead.bitcast(F32),
                                  ALU.subtract).then_inc(drained[s % SIDE_BANKS], 1)

            def side_work(l, what, mixer, g):
                m = step0(mixer, g)
                n0 = first_block(mixer, g)
                if what == "scores":
                    for h in range(HPB):
                        s = m + 2 * TILES + h
                        dve.wait_ge(*step_ready(l, s))
                        if mixer == "attention":
                            dve.scalar_tensor_tensor(probs[:, h, :], side(s)[:, 0:3 * P], P ** -0.5,
                                                     const("log_count"), ALU.mult, ALU.add).then_inc(drained[s % SIDE_BANKS], 1)
                        else:
                            dve.tensor_tensor(probsT[:, h, :], side(s)[:, 0:3 * P], const("causal"),
                                              ALU.mult).then_inc(drained[s % SIDE_BANKS], 1)
                    if mixer == "attention":
                        for h in range(HPB):
                            dve.wait_ge(*step_drained(l, m + 2 * TILES + h))
                            dve.tensor_reduce(neg_max[:, TILES * h:TILES * h + 1], probs[:, h, 0:P], AX_X,
                                              ALU.max, negate=True)
                            last = dve.tensor_reduce(neg_max[:, TILES * h + 1:TILES * h + 2],
                                                     probs[:, h, P:3 * P], AX_X, ALU.max, negate=True)
                        last.then_inc(neg_max_ready, 1)
                elif what == "sums":
                    dve.wait_ge(exp_ready, l * (HPB * GROUPS) + HPB * (g + 1))
                    dve.reciprocal(row_inv, row_sum).then_inc(inv_ready, 1)
                elif what == "values" and mixer == "attention":
                    s0 = m + STEPS[mixer] - TILES - HPB // 2
                    dve.wait_ge(inv_ready, l * GROUPS + (g + 1))
                    dve.wait_ge(*moved_out(l, n0 + 3))
                    for i in range(HPB // 2):
                        dve.wait_ge(*step_ready(l, s0 + i))
                        for hh in range(2):
                            for t in range(TILES):
                                h = 2 * i + hh
                                last = dve.scalar_tensor_tensor(
                                    z_sb[:, t, head(h)], side(s0 + i)[:, head(2 * hh + t)],
                                    row_inv[:, TILES * h + t:TILES * h + t + 1], z_sb[:, t, head(h)],
                                    ALU.mult, ALU.mult)
                        last.then_inc(drained[(s0 + i) % SIDE_BANKS], 1)
                elif what == "values":
                    s0 = m + STEPS[mixer] - TILES - HPB // 2
                    for i in range(HPB // 2):
                        h = HPB * g + 2 * i
                        gq = gamma_q[:, h:h + 2, :].unsqueeze(3).to_broadcast((P, 2, TILES, P))
                        dve.wait_ge(*step_ready(l, s0 + i))
                        dve.tensor_tensor(ret_o[:, 2 * i:2 * i + 2, :, :],
                                          side(s0 + i)[:, :].rearrange("p (h t e) -> p h t e", h=2, t=TILES), gq,
                                          ALU.mult).then_inc(drained[(s0 + i) % SIDE_BANKS], 1)
                elif what == "norm":
                    dve.wait_ge(o_squared, l * GROUPS + (g + 1))
                    dve.tensor_reduce(o_ssq, q_sb[:, :, :].rearrange("p a (b e) -> p (a b) e", e=P), AX_X,
                                      ALU.add).then_inc(o_ssq_ready, 1)
                elif what == "gate" and mixer == "retention":
                    dve.wait_ge(o_rstd_ready, l * GROUPS + (g + 1))
                    dve.wait_ge(*moved_out(l, n0 + 3))
                    for h in range(HPB):
                        for t in range(TILES):
                            last = dve.scalar_tensor_tensor(
                                z_sb[:, t, head(h)], ret_o[:, h, t, :],
                                o_rstd[:, TILES * h + t:TILES * h + t + 1], z_sb[:, t, head(h)],
                                ALU.mult, ALU.mult)
                    last.then_inc(ret_gated, 1)
                elif what == "gate":
                    dve.wait_ge(*moved_out(l, n0 + 2))
                    dve.wait_ge(*moved_out(l, n0 + 3))
                    for t in range(TILES):
                        dve.tensor_tensor(z_sb[:, t, :], z_sb[:, t, :], k_sb[:, t, :],
                                          ALU.mult).then_inc(conv_gated, 1)
                elif what in ("conv0", "conv1", "conv2"):
                    i = int(what[-1])
                    if i == 0:
                        for t in range(TILES):
                            dve.wait_ge(*step_drained(l, m + t))
                    for c in range(HPB):
                        ch = HPB * g + c
                        src = prodT[:, c, 2 - i:2 - i + SEQ]
                        w = tap[2 - i][:, ch:ch + 1]
                        if i == 0:
                            dve.tensor_scalar(kT[:, c, :], src, w, conv_bias[:, ch:ch + 1], ALU.mult,
                                              ALU.add).then_inc(conv_steps, 1)
                        else:
                            dve.wait_ge(conv_steps, l * (3 * HPB * GROUPS) + (HPB * (3 * g + i - 1) + c + 1))
                            dve.scalar_tensor_tensor(kT[:, c, :], src, w, kT[:, c, :], ALU.mult,
                                                     ALU.add).then_inc(conv_steps, 1)
                elif what == "out":
                    s0 = m + STEPS[mixer] - TILES
                    for t in range(TILES):
                        s = s0 + t
                        if mixer == "conv":
                            dve.wait_ge(*step_ready(l, s))
                            if t == 0:
                                dve.wait_ge(conv_steps, l * (3 * HPB * GROUPS) + 3 * HPB * (g + 1))
                            dve.tensor_tensor(heads4(work2[:, t, :]), heads4(side(s)[:, :]), kT[:, :, tok(t)],
                                              ALU.mult).then_inc(drained[s % SIDE_BANKS], 1)
                    for t in range(TILES):
                        lead = oT_lead[:, HPB * g:HPB * (g + 1), tok(t)]
                        dst = oT_trail[:, HPB * g:HPB * (g + 1), tok(t)]
                        if mixer == "conv":
                            dve.wait_ge(*lead_steps(l, lead_no(mixer, g, t)))
                            dve.tensor_tensor(dst, heads4(work2[:, t, :]), lead.bitcast(F32),
                                              ALU.subtract).then_inc(conv_trail, 1)
                        else:
                            trail_of_step(l, s0 + t, lead_no(mixer, g, t), lead, dst)

            def x_trail_of(l, m):
                j, t = divmod(m, TILES)
                dve.wait_ge(x_lead, l * X_STEPS + (m + 1))
                for i in range(HPB):
                    k = HPB * j + i
                    last = dve.scalar_tensor_tensor(hT_trail[:, k, tok(t)], side(m)[:, head(i)],
                                                    pre_gain[:, k:k + 1], hT_lead[:, k, tok(t)].bitcast(F32),
                                                    ALU.mult, ALU.subtract)
                last.then_inc(drained[m % SIDE_BANKS], 1)

            dve.sem_inc(trail_ready, 2 * RAW_SLOTS)
            dve.sem_inc(half_done, SPLIT_SLOTS)
            for e in evicted:
                dve.sem_inc(e, TILES)
            for d in drained:
                dve.sem_inc(d, 1)
            dve.memset(y_rstd, 0.0)
            dve.memset(merged[:, :, :], 0.0).then_inc(y_rstd_ready, 1)
            dve.wait_ge(zeroed, 2)

            def add_y(l, j):
                cols = slice(COLS * j, COLS * (j + 1))
                dve.wait_ge(residual_in[j], l * 16 + 16)
                for t in range(TILES):
                    dve.scalar_tensor_tensor(gates[:, t, cols], merged[:, t, cols], y_rstd[:, t:t + 1],
                                             gates[:, t, cols], ALU.mult, ALU.add).then_inc(x_new, 1)

            with dve.Fori(0, DEPTH) as l:
                dve.wait_ge(y_rstd_ready, l + 1)
                for j in range(OUT_BLOCKS):
                    add_y(l, j)
                    for h in split_before(j):
                        split_trail(l, h)
                    for t in range(TILES):
                        x_trail_of(l, TILES * j + t)
                for h in range(X_HALVES, HALVES + AHEAD):
                    if h < HALVES:
                        split_trail(l, h)
                    if h == SQUARES_FROM + OUT_BLOCKS:
                        dve.wait_ge(x_squared, l * X_STEPS + X_STEPS)
                        dve.tensor_reduce(x_sum, x_ssq.rearrange("p (t j) -> p t j", t=TILES), AX_X,
                                          ALU.add).then_inc(x_sum_ready, 1)
                    if h in EVICT_DUE:
                        evict(l, EVICT_DUE[h])
                    for what, mixer, g in DVE_DUE.get(h, []):
                        side_work(l, what, mixer, g)
                    if h in MERGE_DRAIN_DUE:
                        j = MERGE_DRAIN_DUE[h]
                        for t in range(TILES):
                            trail_of_step(l, MERGE_STEP0 + TILES * j + t, merge_lead_no(j, t),
                                          hT_lead[:, HPB * j:HPB * (j + 1), tok(t)],
                                          hT_trail[:, HPB * j:HPB * (j + 1), tok(t)])
            dve.wait_ge(y_rstd_ready, DEPTH + 1)
            for j in range(OUT_BLOCKS):
                add_y(DEPTH, j)


def constants():
    tq, tk = np.arange(SEQ)[:, None], np.arange(SEQ)[None, :]
    held = np.zeros((SEQ, SEQ))
    for window, dil in DILATIONS:
        held += (tq >= tk) & ((tq - tk) % dil == 0) & (tq - tk <= window)
    log_count = np.where(held > 0, np.log(np.maximum(held, 1.0)), -1e30)
    causal = (tk >= tq).astype(np.float64)
    parts = {
        "ident": np.eye(P),
        "log_count": np.concatenate([log_count[:P, :P], log_count[P:, :]], 1),
        "causal": np.concatenate([causal[:P, :], causal[P:, P:]], 1),
    }
    half = P // 2
    freq = (np.float32(ROPE_BASE) ** (-np.arange(half, dtype=np.float32) / np.float32(half))).astype(np.float32)
    angle = (np.arange(SEQ, dtype=np.float32)[:, None] * freq[None, :]).astype(np.float64)
    by_tile = lambda a: a.reshape(TILES, P, -1).transpose(1, 0, 2).reshape(P, -1)
    parts["cos"], parts["sin"] = by_tile(np.cos(angle)), by_tile(np.sin(angle))
    parts["neg_sin"] = -parts["sin"]
    log_gamma = np.log1p(-np.exp2(-5.0 - np.arange(HEADS)))
    decay = np.arange(SEQ).reshape(TILES, P).T[:, None, :] * log_gamma[None, :, None]
    parts["gamma_q"] = np.exp(decay).reshape(P, -1)
    parts["gamma_v"] = (np.exp(-decay) * P ** -0.5).reshape(P, -1)
    return np.concatenate([parts[n] for n, _ in CONST_PARTS], 1).astype(np.float32)


def kernel(x, pre_norm_g, post_norm_g, w_in, conv_w, conv_b, w_branch_a, w_branch_c, w_branch_r, w_out):
    import concourse.bacc as bacc
    from concourse.bass_utils import run_bass_kernel_spmd

    def by_channel(a):
        a = np.asarray(a)
        return a.reshape(DEPTH, -1, P).transpose(2, 0, 1)

    params = np.concatenate([by_channel(pre_norm_g), by_channel(conv_w), by_channel(conv_b)], 2)
    arrays = {
        "x": np.asarray(x).reshape(SEQ, D_MODEL),
        "w_in": w_in, "w_branch_a": w_branch_a, "w_branch_c": w_branch_c, "w_branch_r": w_branch_r,
        "w_out": w_out, "post_norm_g": post_norm_g,
        "params": params.reshape(P, DEPTH * PARAM_COLS),
        "constants": constants(),
    }
    arrays = {k: np.ascontiguousarray(v) for k, v in arrays.items()}
    nc = bacc.Bacc("TRN2", target_bir_lowering=False, num_devices=1)
    aps = [nc.dram_tensor(k, v.shape, mybir.dt.from_np(v.dtype), kind="ExternalInput").ap()
           for k, v in arrays.items()]
    out = nc.dram_tensor("out", (SEQ, D_MODEL), F32, kind="ExternalOutput").ap()
    build(nc, *aps, out)
    result = run_bass_kernel_spmd(nc, [arrays], core_ids=[0])
    return result.results[0]["out"].reshape(1, SEQ, D_MODEL)
```
